# Optimizing a Trainium2 kernel written in Bass

```python
import jax, jax.numpy as jnp
from jax import lax
import numpy as np

D_MODEL = 1024
BATCH = 1
SEQ = 512
DEPTH = 2
DEC_BATCH = 1
DEC_SEQ = 32
PAST_LEN = 256

CHUNK = 64
HEAD_DIM = 64
ROPE_THETA = 500000.0
NORM_EPS = 1e-6
NEG_INF = -1e30
Q_BLOCK = 128
A_HEADS = 8
A_Q_LORA = 256
A_KV_LORA = 128
A_NOPE = 64
A_ROPE = 32
A_QK = A_NOPE + A_ROPE
A_V = 64
A_SCALE = A_QK ** -0.5
B_HEADS = 8
B_BACK_CHUNKS = 8
B_REACH = B_BACK_CHUNKS * CHUNK
B_MAX_REL = 128
C_HEADS = 16
C_KV_HEADS = 2
C_WINDOW = 128
C_ROT = HEAD_DIM // 4
HEAD_SCALE = HEAD_DIM ** -0.5
D_FF = 2816
N_EVEN = (DEPTH + 1) // 2
N_ODD = DEPTH // 2
EVEN_IN = A_Q_LORA + A_KV_LORA + A_ROPE + 3 * B_HEADS * HEAD_DIM
MIX_EVEN = A_HEADS * A_V + B_HEADS * HEAD_DIM
ODD_IN = (C_HEADS + 2 * C_KV_HEADS) * HEAD_DIM
MIX_ODD = C_HEADS * HEAD_DIM

kernel_name = "hybrid_streaming_encoder_step"

def rms_norm(x, g):
    xf = x.astype(jnp.float32)
    y = xf * lax.rsqrt(jnp.mean(xf * xf, axis=-1, keepdims=True) + NORM_EPS)
    return (y * g.astype(jnp.float32)).astype(x.dtype)

def rope(x, pos, n_rot):
    half = n_rot // 2
    inv = ROPE_THETA ** (-jnp.arange(half, dtype=jnp.float32) / half)
    ang = pos.astype(jnp.float32)[:, None] * inv[None, :]
    cos = jnp.cos(ang)[:, None, :]
    sin = jnp.sin(ang)[:, None, :]
    xf = x.astype(jnp.float32)
    x1, x2 = xf[..., :half], xf[..., half:n_rot]
    out = jnp.concatenate([x1 * cos - x2 * sin, x2 * cos + x1 * sin, xf[..., n_rot:]], axis=-1)
    return out.astype(x.dtype)

def swiglu(x, w_gate, w_up, w_down):
    a = jnp.einsum('btd,df->btf', x, w_gate)
    b = jnp.einsum('btd,df->btf', x, w_up)
    return jnp.einsum('btf,fd->btd', jax.nn.silu(a) * b, w_down)

def attn_probs(s, mask, sink=None):
    s = jnp.where(mask, s, NEG_INF)
    if sink is not None:
        sk = jnp.broadcast_to(sink.astype(jnp.float32)[None, :, None, None], s.shape[:-1] + (1,))
        return jax.nn.softmax(jnp.concatenate([s, sk], axis=-1), axis=-1)[..., :-1]
    return jax.nn.softmax(s, axis=-1)

def mla_attend(qn, qp, k_nope, kpe, v, mask):
    b, q = qn.shape[:2]
    s = jnp.einsum('bqhd,bkhd->bhqk', qn, k_nope) + jnp.einsum('bqhd,bkd->bhqk', qp, kpe)
    p = attn_probs(s.astype(jnp.float32) * A_SCALE, mask)
    return jnp.einsum('bhqk,bkhd->bqhd', p.astype(v.dtype), v).reshape(b, q, A_HEADS * A_V)

def mla_prompt(qn, qp, k_nope, kpe, v):
    b, s_len = qn.shape[:2]
    key_chunk = jnp.arange(s_len) // CHUNK

    def one_block(i):
        start = i * Q_BLOCK
        qnb = lax.dynamic_slice_in_dim(qn, start, Q_BLOCK, axis=1)
        qpb = lax.dynamic_slice_in_dim(qp, start, Q_BLOCK, axis=1)
        q_chunk = (start + jnp.arange(Q_BLOCK)) // CHUNK
        mask = key_chunk[None, :] <= q_chunk[:, None]
        return mla_attend(qnb, qpb, k_nope, kpe, v, mask)

    out = lax.map(one_block, jnp.arange(s_len // Q_BLOCK))
    return jnp.moveaxis(out, 0, 1).reshape(b, s_len, -1)

def band_attend(q, k, v, q_pos, k_pos, rel_table):
    b, nq, h, d = q.shape
    rel = jnp.clip(q_pos[:, None] - k_pos[None, :], -B_MAX_REL, B_MAX_REL) + B_MAX_REL
    bias = rel_table.astype(jnp.float32)[:, rel]
    s = jnp.einsum('bqhd,bkhd->bhqk', q, k).astype(jnp.float32) * HEAD_SCALE + bias[None]
    p = attn_probs(s, (k_pos >= 0)[None, :])
    return jnp.einsum('bhqk,bkhd->bqhd', p.astype(v.dtype), v).reshape(b, nq, h * d)

def swa_attend(q, k, v, k_pos, sinks):
    b, nq, h, d = q.shape
    kvh = k.shape[2]
    g = h // kvh
    nk = k.shape[1]
    qg = q.reshape(b, nq, kvh, g, d)
    s = jnp.einsum('bqkgd,bskd->bkgqs', qg, k).astype(jnp.float32).reshape(b, h, nq, nk) * HEAD_SCALE
    p = attn_probs(s, (k_pos >= 0)[None, :], sinks).reshape(b, kvh, g, nq, nk)
    return jnp.einsum('bkgqs,bskd->bqkgd', p.astype(v.dtype), v).reshape(b, nq, h * d)

def sweep_chunks(attend, q, k, v, reach):
    b, s_len = q.shape[:2]
    pad = ((0, 0), (reach, 0), (0, 0), (0, 0))
    kp, vp = jnp.pad(k, pad), jnp.pad(v, pad)
    band = reach + CHUNK

    def one_chunk(c):
        start = c * CHUNK
        qc = lax.dynamic_slice_in_dim(q, start, CHUNK, axis=1)
        kc = lax.dynamic_slice_in_dim(kp, start, band, axis=1)
        vc = lax.dynamic_slice_in_dim(vp, start, band, axis=1)
        q_pos = start + jnp.arange(CHUNK)
        k_pos = start - reach + jnp.arange(band)
        return attend(qc, kc, vc, q_pos, k_pos)

    out = lax.map(one_chunk, jnp.arange(s_len // CHUNK))
    return jnp.moveaxis(out, 0, 1).reshape(b, s_len, -1)

def even_mixer(h, pos, i, w, cache):
    b, t, _ = h.shape
    proj = jnp.einsum('btd,dc->btc', h, w['even_w_in'][i])
    c0 = A_Q_LORA
    c1 = c0 + A_KV_LORA
    c2 = c1 + A_ROPE
    cq = rms_norm(proj[..., :c0], w['mla_q_norm'][i])
    ckv = rms_norm(proj[..., c0:c1], w['mla_kv_norm'][i])
    kpe = rope(proj[:, :, None, c1:c2], pos, A_ROPE)[:, :, 0, :]
    qkv_b = proj[..., c2:].reshape(b, t, 3, B_HEADS, HEAD_DIM)
    q_b, k_b, v_b = qkv_b[:, :, 0], qkv_b[:, :, 1], qkv_b[:, :, 2]
    q_a = jnp.einsum('btr,rc->btc', cq, w['mla_w_uq'][i]).reshape(b, t, A_HEADS, A_QK)
    qn = q_a[..., :A_NOPE]
    qp = rope(q_a[..., A_NOPE:], pos, A_ROPE)
    w_ukv = w['mla_w_ukv'][i]
    rel_table = w['band_rel_bias'][i]
    band_fn = lambda qc, kc, vc, qpos, kpos: band_attend(qc, kc, vc, qpos, kpos, rel_table)
    if cache is None:
        kv = jnp.einsum('btr,rc->btc', ckv, w_ukv).reshape(b, t, A_HEADS, A_NOPE + A_V)
        out_a = mla_prompt(qn, qp, kv[..., :A_NOPE], kpe, kv[..., A_NOPE:])
        out_b = sweep_chunks(band_fn, q_b, k_b, v_b, B_REACH)
        keep = min(B_REACH, t)
        new = (ckv, kpe, k_b[:, t - keep:], v_b[:, t - keep:])
    else:
        c_ckv, c_kpe, c_k, c_v = cache
        ckv_all = jnp.concatenate([c_ckv, ckv], axis=1)
        kpe_all = jnp.concatenate([c_kpe, kpe], axis=1)
        n_all = ckv_all.shape[1]
        kv = jnp.einsum('btr,rc->btc', ckv_all, w_ukv).reshape(b, n_all, A_HEADS, A_NOPE + A_V)
        out_a = mla_attend(qn, qp, kv[..., :A_NOPE], kpe_all, kv[..., A_NOPE:], jnp.ones((t, n_all), bool))
        nb = c_k.shape[1]
        k_pos = pos[0] - nb + jnp.arange(nb + t)
        out_b = band_fn(q_b, jnp.concatenate([c_k, k_b], axis=1), jnp.concatenate([c_v, v_b], axis=1), pos, k_pos)
        new = (ckv, kpe, k_b, v_b)
    out = jnp.concatenate([out_a, out_b], axis=-1)
    return jnp.einsum('btc,cd->btd', out, w['even_w_out'][i]), new

def odd_mixer(h, pos, i, w, cache):
    b, t, _ = h.shape
    proj = jnp.einsum('btd,dc->btc', h, w['odd_w_in'][i])
    nq = C_HEADS * HEAD_DIM
    nk = C_KV_HEADS * HEAD_DIM
    q = rope(proj[..., :nq].reshape(b, t, C_HEADS, HEAD_DIM), pos, C_ROT)
    k = rope(proj[..., nq:nq + nk].reshape(b, t, C_KV_HEADS, HEAD_DIM), pos, C_ROT)
    v = proj[..., nq + nk:].reshape(b, t, C_KV_HEADS, HEAD_DIM)
    sinks = w['swa_sinks'][i]
    swa_fn = lambda qc, kc, vc, qpos, kpos: swa_attend(qc, kc, vc, kpos, sinks)
    if cache is None:
        out = sweep_chunks(swa_fn, q, k, v, C_WINDOW)
        keep = min(C_WINDOW, t)
        new = (k[:, t - keep:], v[:, t - keep:])
    else:
        c_k, c_v = cache
        nc = c_k.shape[1]
        k_pos = pos[0] - nc + jnp.arange(nc + t)
        out = swa_fn(q, jnp.concatenate([c_k, k], axis=1), jnp.concatenate([c_v, v], axis=1), pos, k_pos)
        new = (k, v)
    return jnp.einsum('btc,cd->btd', out, w['odd_w_out'][i]), new

def trunk(x, pos, caches, w):
    new = ([], [], [], [], [], [])
    for l in range(DEPTH):
        g = w['norm_g'][l]
        ff_a = swiglu(rms_norm(x, g[0]), w['ffn_w_gate'][l, 0], w['ffn_w_up'][l, 0], w['ffn_w_down'][l, 0])
        x = x + 0.5 * rms_norm(ff_a, g[1])
        h = rms_norm(x, g[2])
        i = l // 2
        if l % 2 == 0:
            lc = None if caches is None else (caches[0][i], caches[1][i], caches[2][i], caches[3][i])
            mix, st = even_mixer(h, pos, i, w, lc)
            for j in range(4):
                new[j].append(st[j])
        else:
            lc = None if caches is None else (caches[4][i], caches[5][i])
            mix, st = odd_mixer(h, pos, i, w, lc)
            new[4].append(st[0])
            new[5].append(st[1])
        x = x + rms_norm(mix, g[3])
        ff_b = swiglu(rms_norm(x, g[4]), w['ffn_w_gate'][l, 1], w['ffn_w_up'][l, 1], w['ffn_w_down'][l, 1])
        x = x + 0.5 * rms_norm(ff_b, g[5])
    return x, [jnp.stack(s, axis=0) for s in new]

def setup_inputs(seed: int = 0) -> dict:
    key = jax.random.key(seed)
    ks = jax.random.split(key, 22)
    nrm = lambda k, shape, s: jax.random.normal(k, shape, jnp.float32) * s
    b_cache = min(B_REACH, PAST_LEN)
    c_cache = min(C_WINDOW, PAST_LEN)
    return {
        'x_prompt': nrm(ks[0], (BATCH, SEQ, D_MODEL), 1.0),
        'x_sample': nrm(ks[1], (DEC_BATCH, DEC_SEQ, D_MODEL), 1.0),
        'cache_mla_ckv': nrm(ks[2], (N_EVEN, DEC_BATCH, PAST_LEN, A_KV_LORA), 1.0),
        'cache_mla_kpe': nrm(ks[3], (N_EVEN, DEC_BATCH, PAST_LEN, A_ROPE), 1.0),
        'cache_band_k': nrm(ks[4], (N_EVEN, DEC_BATCH, b_cache, B_HEADS, HEAD_DIM), 1.0),
        'cache_band_v': nrm(ks[5], (N_EVEN, DEC_BATCH, b_cache, B_HEADS, HEAD_DIM), 1.0),
        'cache_swa_k': nrm(ks[6], (N_ODD, DEC_BATCH, c_cache, C_KV_HEADS, HEAD_DIM), 1.0),
        'cache_swa_v': nrm(ks[7], (N_ODD, DEC_BATCH, c_cache, C_KV_HEADS, HEAD_DIM), 1.0),
        'norm_g': 1.0 + nrm(ks[8], (DEPTH, 6, D_MODEL), 0.02),
        'ffn_w_gate': nrm(ks[9], (DEPTH, 2, D_MODEL, D_FF), D_MODEL ** -0.5),
        'ffn_w_up': nrm(ks[10], (DEPTH, 2, D_MODEL, D_FF), D_MODEL ** -0.5),
        'ffn_w_down': nrm(ks[11], (DEPTH, 2, D_FF, D_MODEL), D_FF ** -0.5),
        'even_w_in': nrm(ks[12], (N_EVEN, D_MODEL, EVEN_IN), D_MODEL ** -0.5),
        'mla_q_norm': 1.0 + nrm(ks[13], (N_EVEN, A_Q_LORA), 0.02),
        'mla_w_uq': nrm(ks[14], (N_EVEN, A_Q_LORA, A_HEADS * A_QK), A_Q_LORA ** -0.5),
        'mla_kv_norm': 1.0 + nrm(ks[15], (N_EVEN, A_KV_LORA), 0.02),
        'mla_w_ukv': nrm(ks[16], (N_EVEN, A_KV_LORA, A_HEADS * (A_NOPE + A_V)), A_KV_LORA ** -0.5),
        'band_rel_bias': nrm(ks[17], (N_EVEN, B_HEADS, 2 * B_MAX_REL + 1), 0.5),
        'even_w_out': nrm(ks[18], (N_EVEN, MIX_EVEN, D_MODEL), MIX_EVEN ** -0.5),
        'odd_w_in': nrm(ks[19], (N_ODD, D_MODEL, ODD_IN), D_MODEL ** -0.5),
        'swa_sinks': nrm(ks[20], (N_ODD, C_HEADS), 1.0),
        'odd_w_out': nrm(ks[21], (N_ODD, MIX_ODD, D_MODEL), MIX_ODD ** -0.5),
    }

def reference(x_prompt, x_sample, cache_mla_ckv, cache_mla_kpe, cache_band_k, cache_band_v,
              cache_swa_k, cache_swa_v, norm_g, ffn_w_gate, ffn_w_up, ffn_w_down, even_w_in,
              mla_q_norm, mla_w_uq, mla_kv_norm, mla_w_ukv, band_rel_bias, even_w_out,
              odd_w_in, swa_sinks, odd_w_out):
    w = dict(norm_g=norm_g, ffn_w_gate=ffn_w_gate, ffn_w_up=ffn_w_up, ffn_w_down=ffn_w_down,
             even_w_in=even_w_in, mla_q_norm=mla_q_norm, mla_w_uq=mla_w_uq, mla_kv_norm=mla_kv_norm,
             mla_w_ukv=mla_w_ukv, band_rel_bias=band_rel_bias, even_w_out=even_w_out,
             odd_w_in=odd_w_in, swa_sinks=swa_sinks, odd_w_out=odd_w_out)
    seq = x_prompt.shape[1]
    past = cache_mla_ckv.shape[2]
    t = x_sample.shape[1]
    pos_p = jnp.arange(seq, dtype=jnp.int32)
    pos_s = past + jnp.arange(t, dtype=jnp.int32)
    y_prompt, st_p = trunk(x_prompt, pos_p, None, w)
    caches = (cache_mla_ckv, cache_mla_kpe, cache_band_k, cache_band_v, cache_swa_k, cache_swa_v)
    y_sample, st_s = trunk(x_sample, pos_s, caches, w)
    ckv_p, kpe_p, bk_p, bv_p, sk_p, sv_p = st_p
    ckv_s, kpe_s, bk_s, bv_s, sk_s, sv_s = st_s
    return (y_prompt, y_sample, ckv_p, kpe_p, bk_p, bv_p, sk_p, sv_p, ckv_s, kpe_s, bk_s, bv_s, sk_s, sv_s)


_drawn_inputs = setup_inputs


def setup_inputs(seed=0):
    import zlib

    import numpy as np

    out = dict(_drawn_inputs(seed))
    spreads = {}
    factors = {'mla_q_norm': 4.647, 'mla_kv_norm': 2.812, 'swa_sinks': 8.0}
    for name, (base, spread) in spreads.items():
        noise = np.random.default_rng([zlib.crc32(name.encode()), seed]).standard_normal(out[name].shape)
        drawn = base * np.exp(spread * noise) if base else spread * noise
        out[name] = __import__('jax').numpy.asarray(drawn.astype(out[name].dtype))
    for name, factor in factors.items():
        out[name] = (out[name] * factor).astype(out[name].dtype)
    return out
```

```python
from contextlib import ExitStack

import numpy as np

import concourse.bass as bass
from concourse import mybir

F32 = mybir.dt.float32
F32R = mybir.dt.float32r
ACT = mybir.ActivationFunctionType
ALU = mybir.AluOpType
AX_X = mybir.AxisListType.X

P = 128
D = 1024
KD = D // P
SEQ, DEC, PAST = 512, 32, 256
T = SEQ + DEC
TH = T // 2
HALF = (slice(0, TH), slice(TH, T))
EPS = 1e-6
FF = 2816
KF = FF // P
DU = KF // 2
UW = DU * P
NEG = -1e30
NH = 8
NOPE, ROPE, HD = 64, 32, 64
QK = NOPE + ROPE
KEYS_A = T + PAST
KEYS_AP = 896
CH, CKV = 16, 2
KEYS_C = T + 128
SK = DEC + PAST
A_SCALE = QK ** -0.5
HEAD_SCALE = HD ** -0.5
REL = 415

SUBS = ("ffn", "even", "ffn", "ffn", "odd", "ffn")
IN_STEPS = {"ffn": KF, "even": 8, "odd": 5}
MID_GROUPS = {"ffn": 0, "even": 2, "odd": 0}
OUT_GROUPS = {"ffn": 8, "even": 4, "odd": 4}
OUT_TILES = {"ffn": KF, "even": 8, "odd": 8}
G0, P0 = [0], [0]
for _s in SUBS:
    G0.append(G0[-1] + IN_STEPS[_s] + MID_GROUPS[_s] + OUT_GROUPS[_s])
    P0.append(P0[-1] + 2 * IN_STEPS[_s])


def std_event(c, post, H):
    if c == 0:
        return H
    return 2 + 4 * (c - 1) + H + (0 if post else 2)


def out_order(kind):
    pairs = [(m, H) for i in range(4) for H in range(2) for m in (2 * i, 2 * i + 1)]
    return pairs if kind == "ffn" else pairs[:8] + [(m, H) for H in range(2) for m in range(4, 8)]


def out_event(s, m, H):
    return 16 * s + out_order(SUBS[s]).index((m, H))


def unit_tiles(g):
    s = max(i for i in range(len(SUBS)) if G0[i] <= g)
    kind, j = SUBS[s], g - G0[s]
    if kind == "ffn":
        return (KD, KD) if j < KF else (DU, DU)
    if kind == "even" and j == 8:
        return 6, 6
    if kind == "even" and j == 9:
        return 8, 4
    return KD, KD


def prompt_items_full():
    return [dict(kind="prompt", h=2 * p + e, i=i, width=P * (i + 1),
                 pieces=[(P * j, P) for j in range(i + 1)],
                 masks=[(slice(0, 64), P * i + 64, P * i + 128)])
            for p in range(4) for e in range(2) for i in range(4)]


def attention_plan(name):
    if name in ("mla", "band"):
        items = prompt_items_full()
        pieces = [(0, P), (P, P), (2 * P, 32)] if name == "mla" else [(32, P), (160, P), (0, 32)]
        items += [dict(kind="sample", h=4 * q, width=SK, pieces=pieces, masks=[]) for q in range(2)]
        first = 0 if name == "mla" else 4
        done = [(8 * p + 7, 5 + p % 2, first + p, 1, SEQ) for p in range(4)] + [(33, 7, first, 4, DEC)]
        return items, done
    items = []
    for u in range(4):
        for e in range(2):
            for i in range(4):
                w = P if i == 0 else 2 * P
                masks = [(slice(0, 64), 64, 128)] if i == 0 else [(slice(0, 64), 192, 256), (slice(64, 128), 0, 64)]
                items.append(dict(kind="prompt", h=4 * u + e, i=i, width=w,
                                  pieces=[(P * j, P) for j in range(2 * w // P)], masks=masks))
    items += [dict(kind="sample", h=4 * q, width=DEC + P, pieces=[(32, P), (0, 32)], masks=[]) for q in range(4)]
    done = []
    for u in range(4):
        done += [(8 * u + 7, 5, 2 * u, 1, SEQ), (8 * u + 7, 6, 2 * u + 1, 1, SEQ)]
    done.append((35, 7, 0, 8, DEC))
    return items, done


ATT = {name: attention_plan(name) for name in ("mla", "band", "swa")}
A0 = {"mla": 0, "band": 34, "swa": 68}
O0 = {"mla": 0, "band": 5, "swa": 10}


def build(nc, ins, outs):
    with ExitStack() as ctx:
        cursor = [(nc.sbuf_base + 31) // 32 * 32]

        def place(name, shape, dt, at=None):
            size = 4 * int(np.prod(shape[1:]))
            offset = cursor[0] if at is None else at
            if at is None:
                cursor[0] += (size + 31) // 32 * 32
            return nc.alloc_sbuf_tensor_at(name, shape, dt, offset=offset)

        x = place("x", [P, KD, T], F32)
        xhi_at = cursor[0]
        xhi = place("xhi", [P, KD, T], F32R)
        xlo = place("xlo", [P, KD, T], F32R)
        y_ffn = place("y_ffn", [P, KD, T], F32, at=xhi_at)
        arena = cursor[0]
        h_hi = place("h_hi", [P, KF, T], F32R)
        h_lo = place("h_lo", [P, KF, T], F32R)
        arena_end = cursor[0]
        squares = place("squares", [P, KD, T], F32, at=arena)
        y_mix = place("y_mix", [P, KD, T], F32, at=arena_end - 4 * KD * T)
        w_raw = place("w_raw", [P, 2, UW], F32)
        w_hi = place("w_hi", [P, 4, UW], F32R)
        w_lo = place("w_lo", [P, 4, UW], F32R)
        rstd = place("rstd", [P, T], F32)
        scratch = place("scratch", [P, 4, TH], F32)
        ones = place("ones", [P, P], F32)
        ident = place("ident", [P, P], F32)
        gains = place("gains", [P, 12, KD], F32)
        post_gains = place("post_gains", [P, 6, KD], F32)
        eps = place("eps", [P, 1], F32)
        lat_gains = place("lat_gains", [P, 3], F32)
        rel_far = place("rel_far", [P, NH], F32)
        soft = place("soft", [P, 4, 8], F32)
        assert cursor[0] <= nc.sbuf_usable_end, (cursor[0], nc.sbuf_usable_end)

        qkvb = place("qkvb", [P, 12, T], F32, at=arena)
        kt_at = arena + 26112
        ktA = place("ktA", [QK, NH, KEYS_A], F32, at=kt_at)
        cq = place("cq", [P, 2, T], F32, at=kt_at)
        ckv = place("ckv", [P, T], F32, at=kt_at + 4352)
        kpe_raw = place("kpe_raw", [P, T], F32, at=kt_at + 6528)
        lat_rstd = place("lat_rstd", [P, 2, T], F32, at=kt_at + 8704)
        ckv_cache = place("ckv_cache", [P, PAST], F32, at=kt_at + 13056)
        qtA = place("qtA", [QK, NH, T], F32, at=arena + 51712)
        va_at = arena + 69120
        vA = place("vA", [P, 7, NH * HD], F32, at=va_at)
        cqn_hi = place("cqn_hi", [P, 2, T], F32R, at=va_at)
        cqn_lo = place("cqn_lo", [P, 2, T], F32R, at=va_at + 4352)
        ropeA = place("ropeA", [P, 2, T], F32, at=va_at + 8704)
        ck_at = arena + 83456
        ckv_hi = place("ckv_hi", [P, KEYS_AP], F32R, at=ck_at)
        ckv_lo = place("ckv_lo", [P, KEYS_AP], F32R, at=ck_at + 3584)
        kpe_all = place("kpe_all", [P, KEYS_A], F32, at=ck_at + 7168)
        swapA = place("swapA", [QK, QK], F32, at=ck_at + 10368)
        probsE = place("probsE", [P, 4, 512], F32, at=ck_at)
        probsTE = place("probsTE", [P, 2, 512], F32, at=ck_at + 8192)
        vB = place("vB", [P, 5, NH * HD], F32, at=kt_at)
        vB_cache = place("vB_cache", [P, 2, NH * HD], F32, at=kt_at + 10240)
        kB_cache = place("kB_cache", [P, 4, PAST], F32, at=kt_at + 14336)
        relB = place("relB", [P, NH, 2 * P], F32, at=kt_at + 18432)
        relS = place("relS", [P, 2, SK], F32, at=kt_at + 26624)
        hankel = place("hankel", [P, NH, 2 * P], F32, at=kt_at + 28928)
        hankelS = place("hankelS", [P, 2, SK], F32, at=kt_at + 37120)
        flips = place("flips", [P, 2, P], F32, at=kt_at + 39424)
        qtC = place("qtC", [P, KD, T], F32, at=arena)
        kC = place("kC", [P, T], F32, at=arena + 17408)
        kdup = place("kdup", [P, CKV, KEYS_C], F32, at=arena + 19584)
        vTC = place("vTC", [P, T], F32, at=arena + 24960)
        vC = place("vC", [P, 5, P], F32, at=arena + 27136)
        vC_cache = place("vC_cache", [P, P], F32, at=arena + 29696)
        ropeC = place("ropeC", [P, 4, T], F32, at=arena + 30208)
        swapC = place("swapC", [P, P], F32, at=arena + 38912)
        probsC = place("probsC", [P, 4, 512], F32, at=arena + 39424)
        probsTC = place("probsTC", [P, 2, 512], F32, at=arena + 47616)
        neg_sink = place("neg_sink", [P, CH + 4], F32, at=arena + 51712)
        sink = place("sink", [P, CH + 4], F32, at=arena + 51808)

        psum = ctx.enter_context(nc.psum_tensor("psum", [P, 8, 512], F32))

        def sem(name):
            return ctx.enter_context(nc.semaphore(name))

        gains_in = sem("gains_in")
        consts_in = sem("consts_in")
        x_in = [sem("x_inA"), sem("x_inB")]
        raw_in = [sem("raw_in0"), sem("raw_in1")]
        w_hi_done = sem("w_hi_done")
        w_lo_done = sem("w_lo_done")
        gains_ready = sem("gains_ready")
        std_ready = sem("std_ready")
        x_ready = sem("x_ready")
        xsq_ready = sem("xsq_ready")
        xhi_ready = sem("xhi_ready")
        xlo_ready = sem("xlo_ready")
        prestat = sem("prestat")
        proj_ready = sem("proj_ready")
        proj_read = sem("proj_read")
        gate_scaled = sem("gate_scaled")
        silu_done = sem("silu_done")
        h_ready = sem("h_ready")
        hhi_ready = sem("hhi_ready")
        hlo_ready = sem("hlo_ready")
        y_ready = sem("y_ready")
        ysq_ready = sem("ysq_ready")
        poststat = sem("poststat")
        dve_step = sem("dve_step")
        even_in = sem("even_in")
        pad_zero = sem("pad_zero")
        lat_sq = sem("lat_sq")
        lat_stat = sem("lat_stat")
        lat_std = sem("lat_std")
        lat_norm = sem("lat_norm")
        lat_hi = sem("lat_hi")
        lat_lo = sem("lat_lo")
        q_raw = sem("q_raw")
        q_copied = sem("q_copied")
        swapped = sem("swapped")
        roped = sem("roped")
        k_ready = sem("k_ready")
        k_copied = sem("k_copied")
        v_ready = sem("v_ready")
        v_copied = sem("v_copied")
        kpe_spread = sem("kpe_spread")
        band_in = sem("band_in")
        band_prep = sem("band_prep")
        band_act = sem("band_act")
        band_dve = sem("band_dve")
        odd_in = sem("odd_in")
        k_doubled = sem("k_doubled")
        c_roped = sem("c_roped")
        c_swapped = sem("c_swapped")
        vc_turned = sem("vc_turned")
        vc_copied = sem("vc_copied")
        sinks_ready = sem("sinks_ready")
        s_ready = sem("s_ready")
        max_ready = sem("max_ready")
        exp_done = sem("exp_done")
        p_ready = sem("p_ready")
        pt_turned = sem("pt_turned")
        pt_ready = sem("pt_ready")
        pv_done = sem("pv_done")
        o_hi = sem("o_hi")
        o_lo = sem("o_lo")
        stored = sem("stored")
        latents_stored = sem("latents_stored")
        y_stored = sem("y_stored")

        block = ctx.enter_context(nc.Block())

        def slot(g, u):
            return 2 * (g % 2) + u

        def y_of(s):
            return y_ffn if SUBS[s] == "ffn" else y_mix

        def pre_gain(c):
            return 6 * (c // 3) + 2 * (c % 3)

        def ffn_no(s):
            return sum(k == "ffn" for k in SUBS[:s])

        def wait_group_used(eng, g):
            s = max(i for i in range(len(SUBS)) if G0[i] <= g)
            kind, j = SUBS[s], g - G0[s]
            if j < IN_STEPS[kind]:
                eng.wait_ge(proj_ready, P0[s] + max(2 * j + 2, 3))
            elif kind == "even" and j == 8:
                eng.wait_ge(q_raw, 2 * NH)
            elif kind == "even" and j == 9:
                eng.wait_ge(v_ready, 7)
            else:
                m = j - IN_STEPS[kind] - MID_GROUPS[kind]
                eng.wait_ge(y_ready, out_event(s, m if kind == "ffn" else 2 * m + 1, 1) + 1)

        def act_split(act, g, par, tiles, used=None):
            for u in range(2):
                act.wait_ge(raw_in[u], 16 * (g + 1))
                if u == 0 and used is not None:
                    used(act)
                n = tiles[u] * P
                nc.scalar.activation(w_hi[:, 2 * par + u, 0:n], w_raw[:, u, 0:n], ACT.Copy).then_inc(w_hi_done, 1)

        def dve_split(dve, g, par, tiles):
            for u in range(2):
                dve.wait_ge(w_hi_done, 2 * g + u + 1)
                n = tiles[u] * P
                nc.vector.tensor_tensor(w_lo[:, 2 * par + u, 0:n], w_raw[:, u, 0:n],
                                        w_hi[:, 2 * par + u, 0:n].bitcast(F32), ALU.subtract).then_inc(w_lo_done, 1)

        def split_group(eng, which, g):
            if g >= G0[-1]:
                return
            if which == "act":
                act_split(eng, g, g % 2, unit_tiles(g), (lambda e: wait_group_used(e, g - 2)) if g >= 2 else None)
            else:
                dve_split(eng, g, g % 2, unit_tiles(g))

        @block.sync
        def _(sp):
            sp.dma_start(gains[:], ins["gains"]).then_inc(gains_in, 16)
            sp.dma_start(x[:, :, HALF[0]], ins["x"][:, :, HALF[0]]).then_inc(x_in[0], 16)
            for u in range(2):
                sp.dma_start(w_raw[:, u, 0:D], ins["w_gate_up"][0, 0, u]).then_inc(raw_in[u], 16)
            sp.dma_start(ones[:], ins["ones"]).then_inc(consts_in, 16)
            sp.dma_start(x[:, :, HALF[1]], ins["x"][:, :, HALF[1]]).then_inc(x_in[1], 16)
            sp.dma_start(ident[:], ins["ident"]).then_inc(consts_in, 16)
            sp.dma_start(lat_gains[:], ins["lat_gains"]).then_inc(consts_in, 16)

            def load(g, u, source, n):
                sp.wait_ge(w_lo_done, 2 * (g - 1) + u + 1)
                sp.dma_start(w_raw[:, u, 0:n], source).then_inc(raw_in[u], 16)

            for s, kind in enumerate(SUBS):
                n = ffn_no(s)
                if kind == "ffn":
                    with sp.Fori(1 if s == 0 else 0, KF) as f:
                        for u in range(2):
                            load(f + G0[s], u, ins["w_gate_up"][n, f, u], D)
                    with sp.Fori(0, KD) as m:
                        for u in range(2):
                            load(m + (G0[s] + KF), u, ins["w_down"][n, m, u], UW)
                else:
                    names = ["even_in"] * 8 + ["mla_up"] * 2 + ["even_out"] * 4 if kind == "even" else \
                        ["odd_in"] * 5 + ["odd_out"] * 4
                    for j, name in enumerate(names):
                        for u in range(2):
                            cols = unit_tiles(G0[s] + j)[u] * P
                            if name == "mla_up":
                                source = ins[("mla_uq", "mla_ukv")[j - 8]]
                                source = source[u] if j == 8 else source[:, 0:D] if u == 0 else source[:, D:D + 512]
                            else:
                                source = ins[name][names[:j].count(name), u]
                            load(G0[s] + j, u, source, cols)
            c = len(SUBS)
            for H in range(2):
                for k in range(KD):
                    sp.wait_ge(x_ready, 16 * (c - 1) + 8 * H + k + 1)
                    sp.dma_start(outs["y"][:, k, HALF[H]], x[:, k, HALF[H]]).then_inc(y_stored, 16)
            sp.wait_ge(y_stored, 16 * 2 * KD)

        def mm3(out, s_hi, s_lo, m_hi, m_lo, first, last):
            nc.tensor.matmul(out, s_hi, m_hi, start=first, stop=False)
            nc.tensor.matmul(out, s_hi, m_lo, start=False, stop=False)
            return nc.tensor.matmul(out, s_lo, m_hi, start=False, stop=last)

        @block.tensor
        def _(pe):
            def in_half(s, g, par, event, H, bank, c=None):
                for u in range(2):
                    pe.wait_ge(w_lo_done, 2 * g + u + 1)
                    for k in range(KD):
                        if c is not None and u == 0:
                            pe.wait_ge(xlo_ready, 16 * c + 8 * H + k + 1)
                        mm = mm3(psum[:, bank + u, 0:TH],
                                 w_hi[:, 2 * par + u, k * P:(k + 1) * P], w_lo[:, 2 * par + u, k * P:(k + 1) * P],
                                 xhi[:, k, HALF[H]], xlo[:, k, HALF[H]], k == 0, k == KD - 1)
                        if c is not None and u == 0:
                            pre_square(c, H, k)
                            if c > 0 and H == 0 and k == 2:
                                post_square(c - 1, KD - 1, 1)
                mm.then_inc(proj_ready, 1)

            def pre_square(c, H, k):
                pe.wait_ge(xsq_ready, 16 * c + 8 * H + k + 1)
                if k == 0 and c > 0:
                    pe.wait_ge(std_ready, std_event(c, True, H) + 1)
                nc.tensor.matmul(psum[:, 6 + H, 0:TH], ones[:], squares[:, k, HALF[H]],
                                 start=k == 0, stop=k == KD - 1).then_inc(prestat, 1)

            def first_steps(s):
                g, c = G0[s], s
                if s > 0:
                    pe.wait_ge(ysq_ready, out_event(s - 1, KD - 2, 1) + 1)
                in_half(s, g, g % 2, P0[s], 0, 0, c)
                if s > 0:
                    pe.wait_ge(std_ready, std_event(c, True, 1) + 1)
                in_half(s, g + 1, (g + 1) % 2, P0[s] + 1, 0, 4)
                if s > 0:
                    pe.wait_ge(ysq_ready, 16 * s)
                in_half(s, g, g % 2, P0[s] + 2, 1, 2, c)
                pe.wait_ge(std_ready, std_event(c, False, 1) + 1)
                in_half(s, g + 1, (g + 1) % 2, P0[s] + 3, 1, 6)

            def out_half(s, g, par, e, H, first, mid):
                ffn = SUBS[s] == "ffn"
                tiles = OUT_TILES[SUBS[s]]
                a_hi, a_lo = (h_hi, h_lo) if ffn else (xhi, xlo)
                for k in range(tiles):
                    if ffn and first and k in (0, KF - 1):
                        pe.wait_ge(hlo_ready, 2 * KF * ffn_no(s) + 2 * (KF - 1) + (H + 1 if k else 0))
                    u, j = (k // DU, k % DU) if ffn else (e, k)
                    if j == 0:
                        pe.wait_ge(w_lo_done, 2 * g + u + 1)
                    w = slice(j * P, (j + 1) * P)
                    mm = mm3(psum[:, 2 * e + H, 0:TH], w_hi[:, 2 * par + u, w], w_lo[:, 2 * par + u, w],
                             a_hi[:, k, HALF[H]], a_lo[:, k, HALF[H]], k == 0, k == tiles - 1)
                    if k == tiles // 2 and mid is not None:
                        mid()
                mm.then_inc(y_ready, 1)

            def post_square(s, m, H, event=None, first=False):
                pe.wait_ge(ysq_ready, (out_event(s, m, H) if event is None else event) + 1)
                nc.tensor.matmul(psum[:, 4 + H, 0:TH], ones[:], scratch[:, 2 * H + m % 2, :],
                                 start=first, stop=True, skip_group_check=True).then_inc(poststat, 1)

            def ffn_pair(s, i, first=False):
                g = G0[s] + KF
                for n, (e, H) in enumerate([(0, 0), (1, 0), (0, 1), (1, 1)]):
                    event = i * 4 + (16 * s + n)
                    if not first:
                        pe.wait_ge(ysq_ready, event - 3)
                    pe_, pH = [(1, 1), (0, 0), (1, 0), (0, 1)][n]
                    mid = None if first and n == 0 else \
                        (lambda: post_square(s, pe_, pH, event - 1, first=first and n in (1, 3)))
                    out_half(s, i * 2 + (g + e), (g + e) % 2, e, H, first and e == 0, mid)

            def out_projection(s):
                if SUBS[s] == "ffn":
                    ffn_pair(s, 0, first=True)
                    with pe.Fori(1, KD // 2) as i:
                        ffn_pair(s, i)
                    return
                g = G0[s + 1] - 4
                before = None
                for m, H in out_order(SUBS[s]):
                    if m >= 2:
                        pe.wait_ge(ysq_ready, out_event(s, m - 2, H) + 1)
                    mid = None if before is None else \
                        (lambda: post_square(s, *before, first=before[0] == 0))
                    out_half(s, g + m // 2, (g + m // 2) % 2, m % 2, H, m == 0, mid)
                    before = (m, H)

            def attention(name):
                items, done = ATT[name]
                base, obase = A0[name], O0[name]
                N = len(items)
                probs, probsT = (probsC, probsTC) if name == "swa" else (probsE, probsTE)

                def scores(n):
                    it, bank = items[n], n % 3
                    if n >= 3:
                        pe.wait_ge(exp_done, base + n - 2)
                    if it["kind"] == "prompt":
                        i, w = it["i"], it["width"]
                        q = slice(P * i, P * (i + 1))
                        if name == "mla":
                            mm = nc.tensor.matmul(psum[:, bank, 0:w], qtA[:, it["h"], q], ktA[:, it["h"], 0:w],
                                                  start=True, stop=True)
                        elif name == "band":
                            r = slice(64 * (it["h"] % 2), 64 * (it["h"] % 2) + 64)
                            mm = nc.tensor.matmul(psum[:, bank, 0:w], qkvb[r, it["h"] // 2, q],
                                                  qkvb[r, 4 + it["h"] // 2, 0:w], start=True, stop=True)
                        else:
                            lo = P * max(i - 1, 0)
                            for d in range(2):
                                h = it["h"] + 2 * d
                                r = slice(64 * (h % 2), 64 * (h % 2) + 64)
                                mm = nc.tensor.matmul(psum[:, bank, d * w:(d + 1) * w], qtC[r, h // 2, q],
                                                      kdup[r, h // 8, lo:lo + w], start=True, stop=True)
                    else:
                        for d in range(4):
                            h = it["h"] + d
                            rows = slice(32 * d, 32 * d + 32)
                            r = slice(64 * (h % 2), 64 * (h % 2) + 64)
                            if name == "mla":
                                mm = nc.tensor.matmul(psum[rows, bank, 0:SK], qtA[:, h, SEQ:T],
                                                      ktA[:, h, SEQ:KEYS_A], start=True, stop=True)
                            elif name == "band":
                                nc.tensor.matmul(psum[rows, bank, 0:DEC], qkvb[r, h // 2, SEQ:T],
                                                 qkvb[r, 4 + h // 2, SEQ:T], start=True, stop=True)
                                mm = nc.tensor.matmul(psum[rows, bank, DEC:SK], qkvb[r, h // 2, SEQ:T],
                                                      kB_cache[r, h // 2, :], start=True, stop=True)
                            else:
                                mm = nc.tensor.matmul(psum[rows, bank, 0:DEC + P], qtC[r, h // 2, SEQ:T],
                                                      kdup[r, h // 8, SEQ:KEYS_C], start=True, stop=True)
                    mm.then_inc(s_ready, 1)

                def turn(n):
                    pe.wait_ge(p_ready, base + n + 1)
                    if n >= 2:
                        pe.wait_ge(pt_ready, base + n - 1)
                    for j, (col, kw) in enumerate(items[n]["pieces"]):
                        mm = nc.tensor.transpose(psum[0:kw, 3 + n % 2, j * P:(j + 1) * P],
                                                 probs[:, n % 4, col:col + kw], ident[:])
                    mm.then_inc(pt_turned, 1)

                def values(n):
                    it = items[n]
                    pe.wait_ge(pt_ready, base + n + 1)
                    if it["kind"] == "prompt":
                        if name == "swa" and n % 8 == 0 and n >= 8:
                            pe.wait_ge(o_lo, obase + 2 * (n // 8))
                        if name != "swa" and n % 8 == 0 and n >= 16:
                            pe.wait_ge(o_lo, obase + n // 8 - 1)
                    if it["kind"] == "prompt":
                        heads = [it["h"], it["h"] + 2] if name == "swa" else [it["h"]]
                        per = len(it["pieces"]) // len(heads)
                        for d, h in enumerate(heads):
                            r0 = 64 * (h % 2)
                            bank = 5 + (d if name == "swa" else (h // 2) % 2)
                            for j in range(per):
                                if name == "mla":
                                    v = vA[:, j, h * HD:(h + 1) * HD]
                                elif name == "band":
                                    v = vB[:, j, h * HD:(h + 1) * HD]
                                else:
                                    v = vC[:, max(it["i"] - 1, 0) + j, (h // 8) * HD:(h // 8 + 1) * HD]
                                p = (d * per + j) * P
                                mm = nc.tensor.matmul(psum[r0:r0 + 64, bank, P * it["i"]:P * (it["i"] + 1)], v,
                                                      probsT[:, n % 2, p:p + P], start=j == 0, stop=j == per - 1)
                    else:
                        for d in range(4):
                            h = it["h"] + d
                            r0, pieces = 64 * (h % 2), it["pieces"]
                            for j, (_, kw) in enumerate(pieces):
                                if name == "mla":
                                    v = vA[0:kw, 4 + j, h * HD:(h + 1) * HD]
                                elif name == "band":
                                    v = (vB_cache[:, j, h * HD:(h + 1) * HD] if kw == P
                                         else vB[0:kw, 4, h * HD:(h + 1) * HD])
                                else:
                                    c0 = (h // 8) * HD
                                    v = vC_cache[:, c0:c0 + HD] if kw == P else vC[0:kw, 4, c0:c0 + HD]
                                mm = nc.tensor.matmul(psum[r0:r0 + 64, 7, DEC * (h // 2):DEC * (h // 2 + 1)], v,
                                                      probsT[0:kw, n % 2, j * P + 32 * d:j * P + 32 * d + 32],
                                                      start=j == 0, stop=j == len(pieces) - 1)
                    mm.then_inc(pv_done, 1)

                for n in range(N + 4):
                    if n < N:
                        scores(n)
                    if 3 <= n < N + 3:
                        turn(n - 3)
                    if n >= 4:
                        values(n - 4)

            def even_middle(s):
                g = G0[s] + 8
                pe.wait_ge(even_in, 16 * 5)

                def query(q):
                    h, H = q // 2, q % 2
                    u, hh = h // 4, h % 4
                    if q == 0:
                        pe.wait_ge(lat_lo, 6)
                        pe.wait_ge(proj_read, P0[s] + 16)
                    if q % 8 == 0:
                        pe.wait_ge(w_lo_done, 2 * g + u + 1)
                    if q >= 4:
                        pe.wait_ge(q_copied, q - 3)
                    for k in range(2):
                        w = slice(k * 4 * QK + hh * QK, k * 4 * QK + (hh + 1) * QK)
                        mm = mm3(psum[0:QK, q % 4, 0:TH], w_hi[:, slot(g, u), w], w_lo[:, slot(g, u), w],
                                 cqn_hi[:, k, HALF[H]], cqn_lo[:, k, HALF[H]], k == 0, k == 1)
                    mm.then_inc(q_raw, 1)

                def swap(j):
                    if j < 2:
                        raw = kpe_raw[0:QK, HALF[j]]
                        pe.wait_ge(lat_std, 2)
                    else:
                        pe.wait_ge(q_copied, j - 1)
                        raw = qtA[:, (j - 2) // 2, HALF[j % 2]]
                    if j >= 4:
                        pe.wait_ge(roped, j - 3)
                    nc.tensor.matmul(psum[0:QK, 4 + j % 4, 0:TH], swapA[:], raw,
                                     start=True, stop=True).then_inc(swapped, 1)

                swap(0)
                swap(1)
                for q in range(2 * NH):
                    query(q)
                    if q >= 1:
                        swap(q + 1)
                swap(2 * NH + 1)
                pe.wait_ge(lat_lo, 7)
                pe.wait_ge(pad_zero, 2)
                pe.wait_ge(w_lo_done, 2 * (g + 1) + 1)
                for j in range(2 * NH):
                    h, c = j // 2, j % 2
                    cols = slice(c * (KEYS_A // 2), (c + 1) * (KEYS_A // 2))
                    if j < 4:
                        pe.wait_ge(q_copied, 2 * NH)
                    else:
                        pe.wait_ge(k_copied, j - 3)
                    w = slice(h * P, (h + 1) * P)
                    mm3(psum[:, j % 4, 0:KEYS_A // 2], w_hi[:, slot(g + 1, 0), w], w_lo[:, slot(g + 1, 0), w],
                        ckv_hi[:, cols], ckv_lo[:, cols], True, True).then_inc(k_ready, 1)
                pe.wait_ge(w_lo_done, 2 * (g + 1) + 2)
                pe.wait_ge(roped, 2 * NH + 2)
                for v in range(7):
                    cols = slice(v * P, (v + 1) * P)
                    if v >= 4:
                        pe.wait_ge(v_copied, v - 3)
                    mm3(psum[:, 4 + v % 4, :], ckv_hi[:, cols], ckv_lo[:, cols],
                        w_hi[:, slot(g + 1, 1), 0:512], w_lo[:, slot(g + 1, 1), 0:512], True, True).then_inc(v_ready, 1)
                pe.wait_ge(k_copied, 2 * NH)
                pe.wait_ge(v_copied, 7)
                pe.wait_ge(kpe_spread, NH)

            def band_ready(s):
                def job(j):
                    if j == 5:
                        pe.wait_ge(band_in, 16 * 12)
                        pe.wait_ge(o_lo, O0["band"])
                    if j >= 8:
                        pe.wait_ge(band_act if j % 2 == 0 else band_dve, (j - 8) // 2 + 1)
                    if j < 5:
                        n = P if j < 4 else DEC
                        for v in range(4):
                            mm = nc.tensor.transpose(psum[0:n, j, v * P:(v + 1) * P],
                                                     qkvb[:, 8 + v, j * P:j * P + n], ident[:])
                    elif j < 9:
                        mm = nc.tensor.matmul(psum[:, j % 8, :], flips[:, 0, :],
                                              hankel[:, 2 * (j - 5):2 * (j - 4), :].rearrange("p h k -> p (h k)"),
                                              start=True, stop=True)
                    else:
                        mm = nc.tensor.matmul(psum[:, j % 8, 0:SK], flips[:, 1, :], hankelS[:, j - 9, :],
                                              start=True, stop=True)
                    mm.then_inc(band_prep, 1)

                pe.wait_ge(exp_done, A0["band"])
                pe.wait_ge(pt_ready, A0["band"])
                for j in range(11):
                    job(j)
                pe.wait_ge(band_act, 6)
                pe.wait_ge(band_dve, 5)

            pe.wait_ge(consts_in, 16 * 3)
            for s, kind in enumerate(SUBS):
                first_steps(s)
                g = G0[s]
                if kind == "ffn":
                    with pe.Fori(1, KF // 2) as i:
                        for e in range(2):
                            for H in range(2):
                                pe.wait_ge(proj_read, i * 4 + (P0[s] + (1, 3, 3, 4)[2 * e + H] - 4))
                                in_half(s, i * 2 + (g + e), (g + e) % 2, None, H, 4 * e + 2 * H)
                elif kind == "even":
                    for f in range(2, 8):
                        for H in range(2):
                            pe.wait_ge(proj_read, P0[s] + ((1, 3)[H] if f == 2 else 2 * f + H - 1))
                            in_half(s, g + f, (g + f) % 2, None, H, 2 * H)
                        if f == 4:
                            pe.wait_ge(proj_read, P0[s] + 4)
                            for H in range(2):
                                pe.wait_ge(lat_sq, 3 * H + 3)
                                for t in range(2):
                                    nc.tensor.matmul(psum[:, 4 + H, 0:TH], ones[:], scratch[:, 2 * H + t, :],
                                                     start=t == 0, stop=t == 1)
                                nc.tensor.matmul(psum[:, 6 + H, 0:TH], ones[:], lat_rstd[:, 1, HALF[H]],
                                                 start=True, stop=True).then_inc(lat_stat, 1)
                    even_middle(s)
                    attention("mla")
                    band_ready(s)
                    attention("band")
                    pe.wait_ge(o_lo, O0["swa"])
                else:
                    def swap_c(j):
                        if j < 2:
                            raw = kC[:, HALF[j]]
                        else:
                            raw = qtC[:, j // 2 - 1, HALF[j % 2]]
                        if j >= 4:
                            pe.wait_ge(c_roped, j - 3)
                        nc.tensor.matmul(psum[:, 4 + j % 4, 0:TH], swapC[:], raw,
                                         start=True, stop=True).then_inc(c_swapped, 1)

                    pe.wait_ge(odd_in, 16 * 6)
                    for f in range(2, 5):
                        for H in range(2):
                            pe.wait_ge(proj_read, P0[s] + ((1, 3)[H] if f == 2 else 2 * f + H - 1))
                            in_half(s, g + f, (g + f) % 2, None, H, 2 * H)
                            if f >= 3:
                                if f == 3 and H == 0:
                                    pe.wait_ge(proj_read, P0[s] + 4)
                                    swap_c(0)
                                    swap_c(1)
                                if f == 3 and H == 1:
                                    for j in range(2, 6):
                                        swap_c(j)
                                if f == 4:
                                    if H == 0:
                                        pe.wait_ge(proj_read, P0[s] + 6)
                                    for j in (6 + 2 * H, 7 + 2 * H):
                                        swap_c(j)
                    pe.wait_ge(proj_read, P0[s] + 10)
                    for j in range(10, 18):
                        swap_c(j)
                    for t in range(4):
                        mm = nc.tensor.transpose(psum[:, 0, t * P:(t + 1) * P], vTC[:, t * P:(t + 1) * P], ident[:])
                    mm.then_inc(vc_turned, 1)
                    nc.tensor.transpose(psum[0:DEC, 1, 0:P], vTC[:, SEQ:T], ident[:]).then_inc(vc_turned, 1)
                    pe.wait_ge(vc_copied, 2)
                    pe.wait_ge(c_roped, 18)
                    pe.wait_ge(k_doubled, 16 * 4)
                    attention("swa")
                    pe.wait_ge(o_lo, O0["swa"] + 9)
                out_projection(s)
            post_square(len(SUBS) - 1, KD - 1, 1)

        def attention_act(act, name):
            items, done = ATT[name]
            base, obase = A0[name], O0[name]
            N = len(items)
            probs, probsT = (probsC, probsTC) if name == "swa" else (probsE, probsTE)

            def exponentials(n):
                it, w = items[n], items[n]["width"]
                act.wait_ge(max_ready, base + n + 1)
                if n >= 4:
                    act.wait_ge(pt_turned, base + n - 3)
                source = probs[:, n % 4] if name == "band" else psum[:, n % 3]
                heads = 2 if name == "swa" and it["kind"] == "prompt" else 1
                scale = 1.0
                for d in range(heads):
                    e = nc.scalar.activation(probs[:, n % 4, d * w:(d + 1) * w], source[:, d * w:(d + 1) * w],
                                             ACT.Exp, bias=soft[:, n % 4, d:d + 1], scale=scale,
                                             accum_out=soft[:, n % 4, 2 + d:3 + d])
                    if name == "swa":
                        c = it["h"] + 2 * d if it["kind"] == "prompt" else CH + it["h"] // 4
                        e = nc.scalar.activation(soft[:, n % 4, 4 + d:5 + d], sink[:, c:c + 1], ACT.Exp,
                                                 bias=soft[:, n % 4, d:d + 1])
                e.then_inc(exp_done, 1)

            def copy_turned(n):
                pieces = items[n]["pieces"]
                act.wait_ge(pt_turned, base + n + 1)
                if n >= 2:
                    act.wait_ge(pv_done, base + n - 1)
                full = sum(kw == P for _, kw in pieces) * P
                e = nc.scalar.activation(probsT[:, n % 2, 0:full], psum[:, 3 + n % 2, 0:full], ACT.Copy)
                if full < len(pieces) * P:
                    e = nc.scalar.activation(probsT[0:32, n % 2, full:full + P], psum[0:32, 3 + n % 2, full:full + P],
                                             ACT.Copy)
                e.then_inc(pt_ready, 1)

            def head_outputs(k):
                n, bank, tile, tiles, cols = done[k]
                act.wait_ge(pv_done, base + n + 1)
                out, src = output_views(tile, tiles, cols, bank, xhi)
                nc.scalar.activation(out, src, ACT.Copy).then_inc(o_hi, 1)

            k = 0
            for n in range(N + 4):
                if 3 <= n < N + 3:
                    copy_turned(n - 3)
                if n < N:
                    exponentials(n)
                while k < len(done) and done[k][0] + 4 <= n:
                    head_outputs(k)
                    k += 1

        def output_views(tile, tiles, cols, bank, to):
            if tiles == 1:
                return to[:, tile, 0:cols], psum[:, bank, 0:cols]
            return (to[:, tile:tile + tiles, SEQ:SEQ + cols],
                    psum[:, bank, 0:tiles * cols].rearrange("p (t c) -> p t c", t=tiles))

        @block.scalar
        def _(act):
            def post_std(c, H):
                act.wait_ge(poststat, out_event(c - 1, KD - 1, H) + 1)
                nc.scalar.activation(rstd[:, HALF[H]], psum[:, 4 + H, 0:TH], ACT.Sqrt, bias=eps[:],
                                     scale=1.0 / D).then_inc(std_ready, 1)

            def pre_std(c, H):
                act.wait_ge(prestat, 16 * c + 8 * H + KD)
                nc.scalar.activation(rstd[:, HALF[H]], psum[:, 6 + H, 0:TH], ACT.Sqrt, bias=eps[:],
                                     scale=1.0 / D).then_inc(std_ready, 1)

            def tile(c, H, k):
                if c == 0:
                    if k == 0:
                        act.wait_ge(x_in[H], 16)
                else:
                    act.wait_ge(x_ready, 16 * (c - 1) + 8 * H + k + 1)
                nc.scalar.activation(squares[:, k, HALF[H]], x[:, k, HALF[H]], ACT.Square).then_inc(xsq_ready, 1)
                nc.scalar.activation(xhi[:, k, HALF[H]], x[:, k, HALF[H]], ACT.Copy,
                                     scale=gains[:, pre_gain(c), k:k + 1]).then_inc(xhi_ready, 1)

            def boundary(c):
                g = G0[c]
                if c == 0:
                    for k in range(KD):
                        tile(c, 0, k)
                    split_group(act, "act", 0)
                    for k in range(KD):
                        tile(c, 1, k)
                    split_group(act, "act", 1)
                    pre_std(c, 0)
                    pre_std(c, 1)
                    return
                s = c - 1
                post_std(c, 0)
                takes = {3: [6], 7: [7]} if SUBS[s] == "ffn" else {-1: [4], 1: [5], 3: [6], 5: [7]}
                split_at = 3 if SUBS[s] == "ffn" else 1
                for k in range(-1, KD):
                    if k >= 0 and c < len(SUBS):
                        tile(c, 0, k)
                    for m in takes.get(k, []):
                        out_result(s, out_event(s, m, 1), m, m % 2, 1)
                    if k == split_at:
                        split_group(act, "act", g)
                post_std(c, 1)
                if c == len(SUBS):
                    return
                split_group(act, "act", g + 1)
                pre_std(c, 0)
                for k in range(KD):
                    tile(c, 1, k)
                pre_std(c, 1)

            def gate_half(n, f, H):
                e = f * 2 + (2 * KF * n + H)
                act.wait_ge(gate_scaled, e + 1)
                nc.scalar.activation(scratch[:, 2 * H, :], scratch[:, 2 * H, :], ACT.Silu).then_inc(silu_done, 1)
                act.wait_ge(h_ready, e + 1)
                nc.scalar.activation(h_hi[:, f, HALF[H]], scratch[:, 2 * H, :], ACT.Copy).then_inc(hhi_ready, 1)

            def gate_first(n, f, H):
                e = 2 * KF * n + 2 * H + f
                act.wait_ge(gate_scaled, e + 1)
                nc.scalar.activation(scratch[:, 2 * H, :], scratch[:, 2 * H, :], ACT.Silu).then_inc(silu_done, 1)
                act.wait_ge(h_ready, e + 1)
                nc.scalar.activation(h_hi[:, f, HALF[H]], scratch[:, 2 * H, :], ACT.Copy).then_inc(hhi_ready, 1)

            def out_result(s, event, m, e, H, first=False):
                act.wait_ge(y_ready, event + 1)
                nc.scalar.activation(y_of(s)[:, m, HALF[H]], psum[:, 2 * e + H, 0:TH], ACT.Copy)
                if not first:
                    act.wait_ge(poststat, event - 3 if not isinstance(event, int) else out_event(s, m - 2, H) + 1)
                nc.scalar.activation(scratch[:, 2 * H + e, :], psum[:, 2 * e + H, 0:TH],
                                     ACT.Square).then_inc(ysq_ready, 1)

            act.wait_ge(gains_ready, 7)
            for s, kind in enumerate(SUBS):
                g, n = G0[s], ffn_no(s)
                boundary(s)
                if kind == "ffn":
                    split_group(act, "act", g + 2)
                    gate_first(n, 0, 0)
                    gate_first(n, 1, 0)
                    gate_first(n, 0, 1)
                    gate_first(n, 1, 1)
                    with act.Fori(1, KF // 2 - 1) as i:
                        for e in range(2):
                            f = i * 2 + e
                            act_split(act, f + (g + 1), (g + e + 1) % 2, (KD, KD),
                                      lambda eng: eng.wait_ge(proj_ready, f * 2 + P0[s]))
                            for H in range(2):
                                gate_half(n, f, H)
                    for f in (KF - 2, KF - 1):
                        split_group(act, "act", g + f + 1)
                        for H in range(2):
                            gate_half(n, f, H)
                    split_group(act, "act", g + KF + 1)
                    for e, H in ((0, 0), (1, 0), (0, 1)):
                        out_result(s, out_event(s, e, H), e, e, H, first=True)
                    split_group(act, "act", g + KF + 2)
                    out_result(s, out_event(s, 1, 1), 1, 1, 1, first=True)
                    with act.Fori(1, KD // 2 - 1) as i:
                        act_split(act, i * 2 + (g + KF + 1), (g + KF + 1) % 2, (DU, DU),
                                  lambda eng: eng.wait_ge(y_ready, i * 4 + 16 * s))
                        for n_, (e, H) in enumerate([(0, 0), (1, 0), (0, 1)]):
                            out_result(s, i * 4 + (16 * s + n_), i * 2 + e, e, H)
                        act_split(act, i * 2 + (g + KF + 2), (g + KF) % 2, (DU, DU),
                                  lambda eng: eng.wait_ge(y_ready, i * 4 + (16 * s + 3)))
                        out_result(s, i * 4 + (16 * s + 3), i * 2 + 1, 1, 1)
                    split_group(act, "act", g + KF + KD - 1)
                    for m in (KD - 2, KD - 1):
                        out_result(s, out_event(s, m, 0), m, m % 2, 0)
                    continue
                if kind == "even":
                    split_group(act, "act", g + 2)
                    for H in range(2):
                        act.wait_ge(proj_read, P0[s] + 2 + 2 * H)
                        for t in range(2):
                            nc.scalar.activation(scratch[:, 2 * H + t, :], cq[:, t, HALF[H]],
                                                 ACT.Square).then_inc(lat_sq, 1)
                        nc.scalar.activation(lat_rstd[:, 1, HALF[H]], ckv[:, HALF[H]], ACT.Square).then_inc(lat_sq, 1)
                    for f in (3, 4, 5):
                        split_group(act, "act", g + f)
                    for H in range(2):
                        act.wait_ge(lat_stat, H + 1)
                        nc.scalar.activation(lat_rstd[:, 0, HALF[H]], psum[:, 4 + H, 0:TH], ACT.Sqrt,
                                             bias=eps[:], scale=1.0 / 256)
                        nc.scalar.activation(lat_rstd[:, 1, HALF[H]], psum[:, 6 + H, 0:TH], ACT.Sqrt,
                                             bias=eps[:], scale=1.0 / 128).then_inc(lat_std, 1)
                    act.wait_ge(even_in, 16 * 5)
                    nc.scalar.activation(ckv_hi[:, T:KEYS_A], ckv_cache[:], ACT.Copy).then_inc(lat_hi, 1)
                    for H in range(2):
                        act.wait_ge(lat_norm, 3 * H + 3)
                        for t in range(2):
                            nc.scalar.activation(cqn_hi[:, t, HALF[H]], cq[:, t, HALF[H]], ACT.Copy).then_inc(lat_hi, 1)
                        nc.scalar.activation(ckv_hi[:, HALF[H]], ckv[:, HALF[H]], ACT.Copy).then_inc(lat_hi, 1)
                    for f in (6, 7, 8):
                        split_group(act, "act", g + f)
                    split_group(act, "act", g + 9)
                    for q in range(2 * NH):
                        act.wait_ge(q_raw, q + 1)
                        nc.scalar.activation(qtA[:, q // 2, HALF[q % 2]], psum[0:QK, q % 4, 0:TH], ACT.Copy,
                                             scale=A_SCALE).then_inc(q_copied, 1)
                    split_group(act, "act", g + 10)
                    for j in range(2 * NH):
                        act.wait_ge(k_ready, j + 1)
                        if j == 0:
                            act.wait_ge(lat_lo, 7)
                            act.wait_ge(roped, 2)
                            act.wait_ge(latents_stored, 16)
                        c = slice((j % 2) * (KEYS_A // 2), (j % 2 + 1) * (KEYS_A // 2))
                        nc.scalar.activation(ktA[0:NOPE, j // 2, c], psum[0:NOPE, j % 4, 0:KEYS_A // 2],
                                             ACT.Copy).then_inc(k_copied, 1)
                    attention_act(act, "mla")
                    for j in range(0, 11, 2):
                        act.wait_ge(band_prep, j + 1)
                        if j < 5:
                            n_ = P if j < 4 else DEC
                            out, src = vB[0:n_, j, :], psum[0:n_, j, :]
                        elif j < 9:
                            out, src = relB[:, 2 * (j - 5):2 * (j - 4), :].rearrange("p h k -> p (h k)"), psum[:, j % 8, :]
                        else:
                            out, src = relS[:, j - 9, :], psum[:, j % 8, 0:SK]
                        nc.scalar.activation(out, src, ACT.Copy).then_inc(band_act, 1)
                    attention_act(act, "band")
                else:
                    for f in (2, 3, 4, 5):
                        split_group(act, "act", g + f)
                    act.wait_ge(vc_turned, 1)
                    nc.scalar.activation(vC[:, 0:4, :].rearrange("p t c -> p (t c)"), psum[:, 0, :],
                                         ACT.Copy).then_inc(vc_copied, 1)
                    act.wait_ge(vc_turned, 2)
                    nc.scalar.activation(vC[0:DEC, 4, :], psum[0:DEC, 1, 0:P], ACT.Copy).then_inc(vc_copied, 1)
                    attention_act(act, "swa")
                    act.wait_ge(stored, 16 * 4)
                og = G0[s + 1] - 4
                for n_, (m, H) in enumerate(out_order(kind)[:12]):
                    if n_ in (0, 4, 8):
                        split_group(act, "act", og + n_ // 4 + 1)
                    out_result(s, out_event(s, m, H), m, m % 2, H, first=m < 2)
            boundary(len(SUBS))

        @block.vector
        def _(dve):
            steps = [0]

            def own(ins):
                ins.then_inc(dve_step, 1)
                steps[0] += 1
                return steps[0]

            def own_wait(n):
                dve.wait_ge(dve_step, n)

            def reciprocal(c, post, H):
                dve.wait_ge(std_ready, std_event(c, post, H) + 1)
                own_wait(own(nc.vector.reciprocal(rstd[:, HALF[H]], rstd[:, HALF[H]])))

            def update(c, H, split_after=None):
                s = c - 1
                y = y_of(s)

                def scaled(k):
                    return own(nc.vector.scalar_tensor_tensor(
                        out=y[:, k, HALF[H]], in0=y[:, k, HALF[H]], scalar=post_gains[:, s, k:k + 1],
                        in1=rstd[:, HALF[H]], op0=ALU.mult, op1=ALU.mult))

                n = scaled(0)
                for k in range(KD):
                    n_next = scaled(k + 1) if k + 1 < KD else None
                    own_wait(n)
                    nc.vector.tensor_tensor(x[:, k, HALF[H]], x[:, k, HALF[H]], y[:, k, HALF[H]],
                                            ALU.add).then_inc(x_ready, 1)
                    n = n_next
                    if c < len(SUBS) and k >= 1:
                        low_part(c, H, k - 1)
                    if k == split_after:
                        split_group(dve, "dve", G0[c])
                if c < len(SUBS):
                    low_part(c, H, KD - 1)

            def boundary(c):
                if c == 0:
                    for k in range(KD):
                        low_part(c, 0, k)
                    split_group(dve, "dve", 0)
                    for k in range(KD):
                        low_part(c, 1, k)
                    split_group(dve, "dve", 1)
                else:
                    reciprocal(c, True, 0)
                    update(c, 0, 4 if SUBS[c - 1] == "ffn" else 2)
                    reciprocal(c, True, 1)
                    split_group(dve, "dve", G0[c] + 1)
                    update(c, 1)
                if c < len(SUBS):
                    reciprocal(c, False, 0)
                    reciprocal(c, False, 1)

            def low_part(c, H, k):
                dve.wait_ge(xhi_ready, 16 * c + 8 * H + k + 1)
                nc.vector.scalar_tensor_tensor(
                    out=xlo[:, k, HALF[H]], in0=x[:, k, HALF[H]], scalar=gains[:, pre_gain(c), k:k + 1],
                    in1=xhi[:, k, HALF[H]].bitcast(F32), op0=ALU.mult, op1=ALU.subtract).then_inc(xlo_ready, 1)

            def gate_part(e, f, H, ready, bank):
                dve.wait_ge(proj_ready, ready)
                if not isinstance(e, int) or e > 0:
                    dve.wait_ge(hlo_ready, e)
                nc.vector.tensor_tensor(scratch[:, 2 * H, :], psum[:, bank, 0:TH], rstd[:, HALF[H]],
                                        ALU.mult).then_inc(gate_scaled, 1)
                nc.vector.tensor_tensor(scratch[:, 2 * H + 1, :], psum[:, bank + 1, 0:TH], rstd[:, HALF[H]],
                                        ALU.mult).then_inc(proj_read, 1)
                dve.wait_ge(silu_done, e + 1)
                dve.wait_ge(proj_read, ready)
                nc.vector.tensor_tensor(scratch[:, 2 * H, :], scratch[:, 2 * H, :], scratch[:, 2 * H + 1, :],
                                        ALU.mult).then_inc(h_ready, 1)
                dve.wait_ge(hhi_ready, e + 1)
                nc.vector.tensor_tensor(h_lo[:, f, HALF[H]], scratch[:, 2 * H, :], h_hi[:, f, HALF[H]].bitcast(F32),
                                        ALU.subtract).then_inc(hlo_ready, 1)

            def rotate(job, rows, raw, raw_bank, table, dest, ready, done):
                a, b = scratch[rows, 2 * (job % 2), :], scratch[rows, 2 * (job % 2) + 1, :]
                dve.wait_ge(ready, job + 1)
                if job >= 2:
                    dve.wait_ge(done, job - 1)
                nc.vector.tensor_tensor(a, raw, table[0], ALU.mult)
                own_wait(own(nc.vector.tensor_tensor(b, psum[rows, raw_bank, 0:TH], table[1], ALU.mult)))
                nc.vector.tensor_tensor(dest, a, b, ALU.add).then_inc(done, 1)

            def attention_dve(name):
                items, done = ATT[name]
                base, obase = A0[name], O0[name]
                N = len(items)
                probs = probsC if name == "swa" else probsE

                def maxima(n):
                    it, w, bank = items[n], items[n]["width"], n % 3
                    dve.wait_ge(s_ready, base + n + 1)
                    heads = 2 if name == "swa" and it["kind"] == "prompt" else 1
                    full = psum[:, bank, 0:heads * w].rearrange("p (d w) -> p d w", d=heads)
                    last = None
                    for rows, lo, hi in it["masks"]:
                        last = own(nc.vector.memset(psum[rows, bank, 0:heads * w].rearrange(
                            "p (d w) -> p d w", d=heads)[:, :, lo:hi], NEG))
                    if last:
                        own_wait(last)
                    source = full
                    if name == "band":
                        if n >= 4:
                            dve.wait_ge(pt_turned, base + n - 3)
                        h = it["h"]
                        if it["kind"] == "prompt":
                            near = max(w - 2 * P, 0)
                            if near:
                                nc.vector.tensor_scalar(probs[:, n % 4, 0:near], psum[:, bank, 0:near], HEAD_SCALE,
                                                        rel_far[:, h:h + 1], ALU.mult, ALU.add)
                            rel = relB[:, h, 2 * P - (w - near):2 * P]
                        else:
                            near, rel = 0, relS[:, h // 4, :]
                        own_wait(own(nc.vector.scalar_tensor_tensor(
                            out=probs[:, n % 4, near:w], in0=psum[:, bank, near:w], scalar=HEAD_SCALE, in1=rel,
                            op0=ALU.mult, op1=ALU.add)))
                        source = probs[:, n % 4, 0:w].rearrange("p (d w) -> p d w", d=1)
                    red = nc.vector.tensor_reduce(soft[:, n % 4, 0:heads], source, AX_X, ALU.max, negate=True)
                    if name == "swa":
                        own_wait(own(red))
                        for d in range(heads):
                            c = it["h"] + 2 * d if it["kind"] == "prompt" else CH + it["h"] // 4
                            red = nc.vector.tensor_tensor(soft[:, n % 4, d:d + 1], soft[:, n % 4, d:d + 1],
                                                          neg_sink[:, c:c + 1], ALU.min)
                    red.then_inc(max_ready, 1)

                def normalise(n):
                    it, w = items[n], items[n]["width"]
                    heads = 2 if name == "swa" and it["kind"] == "prompt" else 1
                    dve.wait_ge(exp_done, base + n + 1)
                    total = soft[:, n % 4, 2:2 + heads]
                    if name == "swa":
                        own_wait(own(nc.vector.tensor_tensor(total, total, soft[:, n % 4, 4:4 + heads], ALU.add)))
                    own_wait(own(nc.vector.reciprocal(soft[:, n % 4, 6:6 + heads], total)))
                    for d in range(heads):
                        p = probs[:, n % 4, d * w:(d + 1) * w]
                        last = nc.vector.tensor_scalar(p, p, soft[:, n % 4, 6 + d:7 + d], None, ALU.mult)
                    last.then_inc(p_ready, 1)

                def head_outputs(k):
                    _, bank, tile, tiles, cols = done[k]
                    dve.wait_ge(o_hi, obase + k + 1)
                    hi, src = output_views(tile, tiles, cols, bank, xhi)
                    lo, _ = output_views(tile, tiles, cols, bank, xlo)
                    nc.vector.tensor_tensor(lo, src, hi.bitcast(F32), ALU.subtract).then_inc(o_lo, 1)

                k = 0
                for n in range(N + 4):
                    if n < N:
                        maxima(n)
                    if 2 <= n < N + 2:
                        normalise(n - 2)
                    while k < len(done) and done[k][0] + 4 <= n:
                        head_outputs(k)
                        k += 1

            nc.vector.memset(eps[:], EPS).then_inc(gains_ready, 1)
            dve.wait_ge(gains_in, 16)
            for s, kind in enumerate(SUBS):
                factor = 0.5 if kind == "ffn" else 1.0
                nc.vector.tensor_scalar(post_gains[:, s, :], gains[:, pre_gain(s) + 1, :], factor, None,
                                        ALU.mult).then_inc(gains_ready, 1)
            dve.wait_ge(gains_ready, 7)
            for s, kind in enumerate(SUBS):
                g, n = G0[s], ffn_no(s)
                boundary(s)
                if kind == "ffn":
                    e0 = 2 * KF * n
                    split_group(dve, "dve", g + 2)
                    gate_part(e0, 0, 0, P0[s] + 1, 0)
                    gate_part(e0 + 1, 1, 0, P0[s] + 2, 4)
                    gate_part(e0 + 2, 0, 1, P0[s] + 3, 2)
                    gate_part(e0 + 3, 1, 1, P0[s] + 4, 6)
                    with dve.Fori(1, KF // 2 - 1) as i:
                        for e in range(2):
                            f = i * 2 + e
                            dve_split(dve, f + (g + 1), (g + e + 1) % 2, (KD, KD))
                            for H in range(2):
                                gate_part(f * 2 + (e0 + H), f, H, f * 2 + (P0[s] + H + 1), 4 * e + 2 * H)
                    for f in (KF - 2, KF - 1):
                        split_group(dve, "dve", g + f + 1)
                        for H in range(2):
                            gate_part(e0 + 2 * f + H, f, H, P0[s] + 2 * f + H + 1, 4 * (f % 2) + 2 * H)
                    split_group(dve, "dve", g + KF + 1)
                    split_group(dve, "dve", g + KF + 2)
                    with dve.Fori(1, KD // 2 - 1) as i:
                        for e in range(2):
                            dve_split(dve, i * 2 + (g + KF + 1 + e), (g + KF + 1 + e) % 2, (DU, DU))
                    split_group(dve, "dve", g + KF + KD - 1)
                    continue

                def project_out(event, f, H, bank, dests):
                    dve.wait_ge(proj_ready, P0[s] + event + 1)
                    nc.vector.tensor_tensor(dests[0][:, HALF[H]], psum[:, bank, 0:TH], rstd[:, HALF[H]], ALU.mult)
                    nc.vector.tensor_tensor(dests[1][:, HALF[H]], psum[:, bank + 1, 0:TH], rstd[:, HALF[H]],
                                            ALU.mult).then_inc(proj_read, 1)

                first = [(0, 0, 0, 0), (1, 1, 0, 4), (2, 0, 1, 2), (3, 1, 1, 6)]
                if kind == "even":
                    dests = [(cq[:, 0], cq[:, 1]), (ckv[:], kpe_raw[:])] + \
                        [(qkvb[:, 2 * j], qkvb[:, 2 * j + 1]) for j in range(6)]
                else:
                    dests = [(kC[:], vTC[:])] + [(qtC[:, 2 * j], qtC[:, 2 * j + 1]) for j in range(4)]
                split_group(dve, "dve", g + 2)
                for event, f, H, bank in first:
                    project_out(event, f, H, bank, dests[f])

                def later(f):
                    for H in range(2):
                        project_out(2 * f + H, f, H, 2 * H, dests[f])

                if kind == "even":
                    for f in (2, 3, 4):
                        split_group(dve, "dve", g + f + 1)
                        later(f)
                    for H in range(2):
                        dve.wait_ge(lat_std, H + 1)
                        own_wait(own(nc.vector.reciprocal(lat_rstd[:, :, HALF[H]], lat_rstd[:, :, HALF[H]])))
                        for t in range(3):
                            v = cq[:, t, HALF[H]] if t < 2 else ckv[:, HALF[H]]
                            nc.vector.scalar_tensor_tensor(
                                out=v, in0=v, scalar=lat_gains[:, t:t + 1], in1=lat_rstd[:, t // 2, HALF[H]],
                                op0=ALU.mult, op1=ALU.mult).then_inc(lat_norm, 1)
                    dve.wait_ge(lat_hi, 1)
                    nc.vector.tensor_tensor(ckv_lo[:, T:KEYS_A], ckv_cache[:], ckv_hi[:, T:KEYS_A].bitcast(F32),
                                            ALU.subtract).then_inc(lat_lo, 1)
                    for H in range(2):
                        dve.wait_ge(lat_norm, 3 * H + 3)
                        dve.wait_ge(lat_hi, 3 * H + 4)
                        for t in range(2):
                            nc.vector.tensor_tensor(cqn_lo[:, t, HALF[H]], cq[:, t, HALF[H]],
                                                    cqn_hi[:, t, HALF[H]].bitcast(F32), ALU.subtract).then_inc(lat_lo, 1)
                        nc.vector.tensor_tensor(ckv_lo[:, HALF[H]], ckv[:, HALF[H]], ckv_hi[:, HALF[H]].bitcast(F32),
                                                ALU.subtract).then_inc(lat_lo, 1)
                    for f in (5, 6, 7):
                        split_group(dve, "dve", g + f + 1)
                        later(f)
                    split_group(dve, "dve", g + 9)
                    dve.wait_ge(even_in, 16 * 5)
                    rows = slice(NOPE, QK)
                    for j in range(2 * NH + 2):
                        H = j % 2
                        raw = kpe_raw[rows, HALF[H]] if j < 2 else qtA[rows, j // 2 - 1, HALF[H]]
                        dest = kpe_all[rows, HALF[H]] if j < 2 else raw
                        rotate(j, rows, raw, 4 + j % 4, (ropeA[rows, 0, HALF[H]], ropeA[rows, 1, HALF[H]]), dest,
                               swapped, roped)
                    split_group(dve, "dve", g + 10)
                    for v in range(7):
                        dve.wait_ge(v_ready, v + 1)
                        if v == 0:
                            dve.wait_ge(roped, 2 * NH + 2)
                        nc.vector.tensor_copy(vA[:, v, :], psum[:, 4 + v % 4, :]).then_inc(v_copied, 1)
                    attention_dve("mla")
                    for j in range(1, 11, 2):
                        dve.wait_ge(band_prep, j + 1)
                        if j < 5:
                            out, src = vB[:, j, :], psum[:, j, :]
                        elif j < 9:
                            out, src = relB[:, 2 * (j - 5):2 * (j - 4), :].rearrange("p h k -> p (h k)"), psum[:, j % 8, :]
                        else:
                            out, src = relS[:, j - 9, :], psum[:, j % 8, 0:SK]
                        nc.vector.tensor_copy(out, src).then_inc(band_dve, 1)
                    dve.wait_ge(band_act, 6)
                    dve.wait_ge(band_dve, 5)
                    attention_dve("band")
                else:
                    def rotate_c(j):
                        H = j % 2
                        raw = kC[:, HALF[H]] if j < 2 else qtC[:, j // 2 - 1, HALF[H]]
                        t = 2 if j < 2 else 0
                        rotate(j, slice(0, P), raw, 4 + j % 4, (ropeC[:, t, HALF[H]], ropeC[:, t + 1, HALF[H]]), raw,
                               c_swapped, c_roped)

                    dve.wait_ge(odd_in, 16 * 6)
                    nc.vector.tensor_scalar(neg_sink[:], sink[:], -1.0, None, ALU.mult).then_inc(sinks_ready, 1)
                    for f in (2, 3, 4):
                        split_group(dve, "dve", g + f + 1)
                        if f == 3:
                            for j in (0, 1):
                                rotate_c(j)
                            project_out(6, 3, 0, 0, dests[3])
                            for j in (2, 3):
                                rotate_c(j)
                            project_out(7, 3, 1, 2, dests[3])
                            for j in (4, 5):
                                rotate_c(j)
                        elif f == 4:
                            for H in range(2):
                                project_out(8 + H, 4, H, 2 * H, dests[4])
                                for j in (6 + 2 * H, 7 + 2 * H):
                                    rotate_c(j)
                        else:
                            later(f)
                    for j in range(10, 18):
                        rotate_c(j)
                    dve.wait_ge(sinks_ready, 1)
                    attention_dve("swa")
                for j in range(1, 4):
                    split_group(dve, "dve", G0[s + 1] - 4 + j)
            boundary(len(SUBS))

        @block.gpsimd
        def _(pool):
            load = nc.gpsimd.dma_start
            s = 1
            pool.wait_ge(y_ready, 16 * s)
            rows = slice(NOPE, QK)
            load(ropeA[rows, :, :], ins["rope_mla"]).then_inc(even_in, 16)
            load(swapA[:], ins["swap_mla"]).then_inc(even_in, 16)
            load(rel_far[:], ins["rel_far"]).then_inc(even_in, 16)
            load(ckv_cache[:], ins["ckv_cache"]).then_inc(even_in, 16)
            load(kpe_all[rows, T:KEYS_A], ins["kpe_cache"]).then_inc(even_in, 16)
            nc.gpsimd.memset(ckv_hi[:, KEYS_A:KEYS_AP].bitcast(F32), 0.0).then_inc(pad_zero, 1)
            nc.gpsimd.memset(ckv_lo[:, KEYS_A:KEYS_AP].bitcast(F32), 0.0).then_inc(pad_zero, 1)
            pool.wait_ge(lat_norm, 6)
            pool.dma_start(outs["ckv"], ckv[:]).then_inc(latents_stored, 16)
            pool.wait_ge(proj_read, P0[s] + 16)
            pool.dma_start(outs["band_kv"], qkvb[:, 4:12, :]).then_inc(stored, 16)
            pool.wait_ge(roped, 2)
            pool.dma_start(outs["kpe"], kpe_all[rows, 0:T]).then_inc(stored, 16)
            pool.wait_ge(lat_lo, 7)
            pool.wait_ge(latents_stored, 16)
            pool.wait_ge(even_in, 16 * 5)
            pool.wait_ge(stored, 32)
            pool.wait_ge(pad_zero, 2)
            for h in range(NH):
                nc.gpsimd.tensor_copy(ktA[rows, h, :], kpe_all[rows, :]).then_inc(kpe_spread, 1)
            pool.wait_ge(s_ready, A0["band"])
            load(vB_cache[:], ins["band_v_cache"]).then_inc(band_in, 16)
            load(kB_cache[:], ins["band_k_cache"]).then_inc(band_in, 16)
            load(flips[:], ins["flips"]).then_inc(band_in, 16)
            rel = ins["rel_rows"]
            load(hankel[:], bass.AP(rel.tensor, rel.offset + 32, [[1, P], [REL, NH], [1, 2 * P]])).then_inc(band_in, 16)
            for d in range(4):
                for cols, start in ((slice(0, DEC), 256), (slice(DEC, SK), 0)):
                    load(hankelS[32 * d:32 * d + 32, :, cols],
                         bass.AP(rel.tensor, rel.offset + d * REL + start,
                                 [[1, DEC], [4 * REL, 2], [1, cols.stop - cols.start]])).then_inc(band_in, 16)
            s = 4
            pool.wait_ge(y_ready, 16 * s)
            load(ropeC[:], ins["rope_swa"]).then_inc(odd_in, 16)
            load(swapC[:], ins["swap_swa"]).then_inc(odd_in, 16)
            load(vC_cache[:], ins["swa_v_cache"]).then_inc(odd_in, 16)
            load(kdup[:, :, T:KEYS_C], ins["swa_k_cache"]).then_inc(odd_in, 16)
            load(sink[:, 0:CH], ins["sinks"]).then_inc(odd_in, 16)
            load(sink[:, CH:CH + 4], ins["sinks_sample"]).then_inc(odd_in, 16)
            pool.wait_ge(proj_read, P0[s] + 4)
            pool.dma_start(outs["swa_v"], vTC[:]).then_inc(stored, 16)
            pool.wait_ge(c_roped, 2)
            for kv in range(CKV):
                for r in range(2):
                    pool.dma_start(kdup[64 * r:64 * r + 64, kv, 0:T], kC[64 * kv:64 * kv + 64, :]).then_inc(k_doubled, 16)
            pool.dma_start(outs["swa_k"], kC[:]).then_inc(stored, 16)
            pool.wait_ge(stored, 16 * 4)


def rotation(half, rows):
    inv = np.float32(500000.0) ** (-np.arange(half, dtype=np.float32) / np.float32(half))
    pos = np.concatenate([np.arange(SEQ), PAST + np.arange(DEC)]).astype(np.float32)
    ang = (pos[None, :] * inv.astype(np.float32)[:, None]).astype(np.float32)
    cos, sin = np.ones((rows, T), np.float32), np.zeros((rows, T), np.float32)
    cos[0:2 * half] = np.tile(np.cos(ang), (2, 1))
    sin[0:2 * half] = np.tile(np.sin(ang), (2, 1))
    return cos, sin


def partner(size, starts, half):
    m = np.zeros((size, size), np.float32)
    for a in starts:
        for i in range(half):
            m[a + half + i, a + i] = -1.0
            m[a + i, a + half + i] = 1.0
    return m


def tiled(w, columns):
    k = w.shape[0] // P
    return w[:, columns].reshape(k, P, -1, P).transpose(2, 1, 0, 3).reshape(-1, P, k * P)


def layouts(i):
    c = np.ascontiguousarray
    a = {}
    tok = np.concatenate([i["x_prompt"][0], i["x_sample"][0]], 0)
    a["x"] = c(tok.T.reshape(KD, P, T).transpose(1, 0, 2))
    a["gains"] = c(i["norm_g"].reshape(12, KD, P).transpose(2, 0, 1))
    a["lat_gains"] = c(np.concatenate([i["mla_q_norm"][0].reshape(2, P), i["mla_kv_norm"]], 0).T)
    a["ones"], a["ident"] = np.ones((P, P), np.float32), np.eye(P, dtype=np.float32)
    gu = [i[n].reshape(4, KD, P, KF, P).transpose(0, 3, 2, 1, 4).reshape(4, KF, P, D)
          for n in ("ffn_w_gate", "ffn_w_up")]
    a["w_gate_up"] = np.stack(gu, 2)
    a["w_down"] = c(i["ffn_w_down"].reshape(4, 2, DU, P, KD, P).transpose(0, 4, 1, 3, 2, 5)).reshape(4, KD, 2, P, UW)
    win = i["even_w_in"][0]
    pad = np.zeros((D, P), win.dtype)
    pad[:, NOPE:QK] = win[:, 384:416]
    wide = np.concatenate([win[:, 0:384], pad, win[:, 416:]], 1)
    a["even_in"] = c(tiled(wide, slice(None)).reshape(8, 2, P, D))
    uq = i["mla_w_uq"][0].reshape(2, P, 2, 4 * QK)
    a["mla_uq"] = c(uq.transpose(2, 1, 0, 3).reshape(2, P, 8 * QK))
    ukv = i["mla_w_ukv"][0]
    a["mla_ukv"] = c(np.concatenate([ukv, ukv.reshape(P, NH, P)[:, :, NOPE:].reshape(P, 512)], 1))
    a["even_out"] = c(tiled(i["even_w_out"][0], slice(None)).reshape(4, 2, P, D))
    wo = i["odd_w_in"][0]
    a["odd_in"] = c(tiled(np.concatenate([wo[:, D:], wo[:, 0:D]], 1), slice(None)).reshape(5, 2, P, D))
    a["odd_out"] = c(tiled(i["odd_w_out"][0], slice(None)).reshape(4, 2, P, D))
    a["ckv_cache"] = c(i["cache_mla_ckv"][0, 0].T)
    a["kpe_cache"] = c(i["cache_mla_kpe"][0, 0].T)
    a["band_k_cache"] = c(i["cache_band_k"][0, 0].reshape(PAST, 4, P).transpose(2, 1, 0))
    a["band_v_cache"] = c(i["cache_band_v"][0, 0].reshape(2, P, NH * HD).transpose(1, 0, 2))
    k = i["cache_swa_k"][0, 0].transpose(1, 2, 0)
    a["swa_k_cache"] = c(np.concatenate([k, k], 1).transpose(1, 0, 2))
    a["swa_v_cache"] = c(i["cache_swa_v"][0, 0].reshape(P, P))
    table = i["band_rel_bias"][0][:, ::-1]
    a["rel_rows"] = c(np.concatenate([np.repeat(table[:, 0:1], 159, 1), table[:, 0:256]], 1))
    a["rel_far"] = c(np.broadcast_to(table[:, 0][None, :], (P, NH)))
    sinks = i["swa_sinks"][0]
    a["sinks"] = c(np.broadcast_to(sinks[None, :], (P, CH)))
    a["sinks_sample"] = c(np.repeat(sinks.reshape(4, 4).T, 32, 0))
    flips = np.zeros((P, 2, P), np.float32)
    flips[:, 0] = np.eye(P)[::-1]
    for d in range(4):
        flips[32 * d:32 * d + 32, 1, 32 * d:32 * d + 32] = np.eye(32)[::-1]
    a["flips"] = flips
    cos, sin = rotation(ROPE // 2, ROPE)
    a["rope_mla"] = c(np.stack([cos, sin], 1))
    cos, sin = (np.tile(t, (2, 1)) for t in rotation(8, HD))
    a["rope_swa"] = c(np.stack([cos * np.float32(HEAD_SCALE), sin * np.float32(HEAD_SCALE), cos, sin], 1))
    a["swap_mla"] = partner(QK, [NOPE], ROPE // 2)
    a["swap_swa"] = partner(P, [0, HD], 8)
    return a


OUT_SHAPES = dict(y=(P, KD, T), ckv=(P, T), kpe=(ROPE, T), band_kv=(P, 8, T), swa_k=(P, T), swa_v=(P, T))


def kernel(**inputs):
    import concourse.bacc as bacc
    from concourse.bass_utils import run_bass_kernel_spmd

    arrays = layouts({k: np.asarray(v) for k, v in inputs.items()})
    nc = bacc.Bacc("TRN2", target_bir_lowering=False, num_devices=1)
    ins = {n: nc.dram_tensor("in_" + n, v.shape, F32, kind="ExternalInput").ap() for n, v in arrays.items()}
    outs = {n: nc.dram_tensor("out_" + n, s, F32, kind="ExternalOutput").ap() for n, s in OUT_SHAPES.items()}
    build(nc, ins, outs)
    r = run_bass_kernel_spmd(nc, [{"in_" + n: v for n, v in arrays.items()}], core_ids=[0]).results[0]
    y = r["out_y"].transpose(2, 1, 0).reshape(T, D)
    ckv, kpe = r["out_ckv"].T, r["out_kpe"].T
    kv = r["out_band_kv"].transpose(2, 1, 0).reshape(T, 2, NH, HD)
    ck, cv = r["out_swa_k"].T.reshape(T, CKV, HD), r["out_swa_v"].T.reshape(T, CKV, HD)
    c = np.ascontiguousarray
    prompt = (ckv[:SEQ], kpe[:SEQ], kv[:SEQ, 0], kv[:SEQ, 1], ck[SEQ - P:SEQ], cv[SEQ - P:SEQ])
    sample = (ckv[SEQ:], kpe[SEQ:], kv[SEQ:, 0], kv[SEQ:, 1], ck[SEQ:], cv[SEQ:])
    return (c(y[:SEQ])[None], c(y[SEQ:])[None], *(c(v)[None, None] for v in prompt + sample))
```

```python
from contextlib import ExitStack

import numpy as np

import concourse.bass as bass
from concourse import mybir

F32 = mybir.dt.float32
F32R = mybir.dt.float32r
ACT = mybir.ActivationFunctionType
ALU = mybir.AluOpType
AX_X = mybir.AxisListType.X

P = 128
D = 1024
KD = D // P
SEQ, DEC, PAST = 512, 32, 256
T = SEQ + DEC
TH = T // 2
HALF = (slice(0, TH), slice(TH, T))
EPS = 1e-6
FF = 2816
KF = FF // P
DU = KF // 2
UW = DU * P
NEG = -1e30
NH = 8
NOPE, ROPE, HD = 64, 32, 64
QK = NOPE + ROPE
KEYS_A = T + PAST
KEYS_AP = 896
CH, CKV = 16, 2
KEYS_C = T + 128
SK = DEC + PAST
A_SCALE = QK ** -0.5
HEAD_SCALE = HD ** -0.5
REL = 415

SUBS = ("ffn", "even", "ffn", "ffn", "odd", "ffn")
IN_STEPS = {"ffn": KF, "even": 8, "odd": 5}
MID_GROUPS = {"ffn": 0, "even": 2, "odd": 0}
EARLY, EARLY_REST = range(KD - 2), range(KD - 2, KD)
OUT_GROUPS = {"ffn": 8, "even": 4, "odd": 4}
OUT_TILES = {"ffn": KF, "even": 8, "odd": 8}
G0, P0 = [0], [0]
for _s in SUBS:
    G0.append(G0[-1] + IN_STEPS[_s] + MID_GROUPS[_s] + OUT_GROUPS[_s])
    P0.append(P0[-1] + 2 * IN_STEPS[_s])


def std_event(c, post, H):
    if c == 0:
        return H
    return 2 + 4 * (c - 1) + H + (0 if post else 2)


def out_order(kind):
    pairs = [(m, H) for i in range(4) for H in range(2) for m in (2 * i, 2 * i + 1)]
    return pairs if kind == "ffn" else pairs[:8] + [(m, H) for H in range(2) for m in range(4, 8)]


def out_event(s, m, H):
    return 16 * s + out_order(SUBS[s]).index((m, H))


def unit_tiles(g):
    s = max(i for i in range(len(SUBS)) if G0[i] <= g)
    kind, j = SUBS[s], g - G0[s]
    if kind == "ffn":
        return (KD, KD) if j < KF else (DU, DU)
    if kind == "even" and j == 8:
        return 6, 6
    if kind == "even" and j == 9:
        return 8, 4
    return KD, KD


def heads_ready(kind, k, H):
    if H:
        return O0["swa"] + (9 if kind == "odd" else 0)
    return O0["swa"] + k + 1 if kind == "odd" else k + (1 if k < 4 else O0["band"] - 3)


def attention_plan(name):
    if name in ("mla", "band"):
        pieces = [(0, P), (P, P), (2 * P, 32)] if name == "mla" else [(32, P), (160, P), (0, 32)]
        items = [dict(kind="prompt", h=2 * p + e, i=i, width=P * (i + 1), block=i, to=[(p, e, 0)],
                      pieces=[(P * j, P) for j in range(i + 1)])
                 for p in range(4) for e in range(2) for i in range(4)]
        items += [dict(kind="sample", h=4 * q, width=SK, pieces=pieces, block=q, to=[(4, 0, 0), (4, 1, 0)])
                  for q in range(2)]
        first = 0 if name == "mla" else 4
        return items, [(8 * p + 7, first + p, 4, "prompt") for p in range(4)] + [(33, first, 2, "sample")]
    items = [dict(kind="prompt", h=4 * u + e, i=i, width=P if i == 0 else 2 * P, block=i,
                  to=[(2 * u, e, 0), (2 * u + 1, e, 1)], pieces=[(P * j, P) for j in range(2 if i == 0 else 4)])
             for u in range(4) for e in range(2) for i in range(4)]
    items += [dict(kind="sample", h=4 * q, width=DEC + P, pieces=[(32, P), (0, 32)], block=q,
                   to=[(8, 0, 0), (8, 1, 0)]) for q in range(4)]
    return items, [(8 * (t // 2) + 7 + 2 * (t % 2), t, 4, "prompt") for t in range(8)] + [(35, 0, 4, "sample")]


ATT = {name: attention_plan(name) for name in ("mla", "band", "swa")}
A0 = {"mla": 0, "band": 34, "swa": 68}
O0 = {"mla": 0, "band": 5, "swa": 10}


def build(nc, ins, outs):
    with ExitStack() as ctx:
        cursor = [(nc.sbuf_base + 31) // 32 * 32]

        def place(name, shape, dt, at=None):
            size = 4 * int(np.prod(shape[1:]))
            offset = cursor[0] if at is None else at
            if at is None:
                cursor[0] += (size + 31) // 32 * 32
            return nc.alloc_sbuf_tensor_at(name, shape, dt, offset=offset)

        x = place("x", [P, KD, T], F32)
        xhi_at = cursor[0]
        xhi = place("xhi", [P, KD, T], F32R)
        xlo_at = cursor[0]
        xlo = place("xlo", [P, KD, T], F32R)
        y_ffn = place("y_ffn", [P, KD, T], F32, at=xhi_at)
        arena = cursor[0]
        h_hi = place("h_hi", [P, KF, T], F32R)
        h_lo = place("h_lo", [P, KF, T], F32R)
        arena_end = cursor[0]
        squares = place("squares", [P, KD, T], F32, at=arena)
        y_mix = place("y_mix", [P, KD, T], F32, at=arena_end - 4 * KD * T)
        w_raw = place("w_raw", [P, 2, UW], F32)
        w_hi = place("w_hi", [P, 4, UW], F32R)
        w_lo = place("w_lo", [P, 4, UW], F32R)
        rstd = place("rstd", [P, T], F32)
        scratch_at = cursor[0]
        scratch = place("scratch", [P, 4, TH], F32)
        osb_at = scratch_at + 1536
        identE = place("identE", [P, P], F32R, at=scratch_at)
        maskE = place("maskE", [P, 2 * P], F32R, at=scratch_at + 512)
        ones = place("ones", [P, P], F32)
        ident = place("ident", [P, P], F32)
        gains = place("gains", [P, 12, KD], F32)
        post_gains = place("post_gains", [P, 6, KD], F32)
        eps = place("eps", [P, 1], F32)
        lat_gains = place("lat_gains", [P, 3], F32)
        rel_far = place("rel_far", [P, NH], F32)
        soft = place("soft", [P, 8, 6], F32)
        assert cursor[0] <= nc.sbuf_usable_end, (cursor[0], nc.sbuf_usable_end)

        qkvb = place("qkvb", [P, 12, T], F32, at=arena)
        kt_at = arena + 26112
        ktA = place("ktA", [QK, NH, KEYS_A], F32, at=kt_at)
        cq = place("cq", [P, 2, T], F32, at=kt_at)
        ckv = place("ckv", [P, T], F32, at=kt_at + 4352)
        kpe_raw = place("kpe_raw", [P, T], F32, at=kt_at + 6528)
        lat_rstd = place("lat_rstd", [P, 2, T], F32, at=kt_at + 8704)
        ckv_cache = place("ckv_cache", [P, PAST], F32, at=kt_at + 13056)
        qtA = place("qtA", [QK, NH, T], F32, at=arena + 51712)
        va_at = arena + 69120
        vA = place("vA", [P, 7, NH * HD], F32, at=va_at)
        cqn_hi = place("cqn_hi", [P, 2, T], F32R, at=va_at)
        cqn_lo = place("cqn_lo", [P, 2, T], F32R, at=va_at + 4352)
        ropeA = place("ropeA", [P, 2, T], F32, at=va_at + 8704)
        ck_at = arena + 83456
        ckv_hi = place("ckv_hi", [P, KEYS_AP], F32R, at=ck_at)
        ckv_lo = place("ckv_lo", [P, KEYS_AP], F32R, at=ck_at + 3584)
        kpe_all = place("kpe_all", [P, KEYS_A], F32, at=ck_at + 7168)
        swapA = place("swapA", [QK, QK], F32, at=ck_at + 10368)
        probsE = place("probsE", [P, 4, 512], F32, at=ck_at)
        probsTE = place("probsTE", [P, 2, 512], F32, at=ck_at + 8192)
        vB = place("vB", [P, 5, NH * HD], F32, at=kt_at)
        vB_cache = place("vB_cache", [P, 2, NH * HD], F32, at=kt_at + 10240)
        kB_cache = place("kB_cache", [P, 4, PAST], F32, at=kt_at + 14336)
        rel_hi = place("rel_hi", [P, NH, 2 * P], F32R, at=kt_at + 18432)
        relS_hi = place("relS_hi", [P, 2, SK], F32R, at=kt_at + 26624)
        rel_lo = place("rel_lo", [P, NH, 2 * P], F32R, at=va_at)
        relS_lo = place("relS_lo", [P, 2, SK], F32R, at=va_at + 8192)
        hankel = place("hankel", [P, NH, 2 * P], F32, at=xhi_at + 4 * 4 * T)
        hankelS = place("hankelS", [P, 2, SK], F32, at=xlo_at + 4 * 4 * T)
        flips = place("flips", [P, 2, P], F32, at=xlo_at + 4 * 4 * T + 2304)
        far4 = place("far4", [P, 2], F32, at=xlo_at + 4 * 4 * T + 3328)
        mask_rawE = place("mask_rawE", [P, 2 * P], F32, at=xlo_at + 4 * 4 * T + 3360)
        osbA = [place("osbA0", [P, 4, P], F32, at=xlo_at + 4 * 4 * T + 4384), place("osbA1", [P, 4, P], F32, at=osb_at)]
        osbB = [place("osbB0", [P, 4, P], F32, at=kt_at + 29184), place("osbB1", [P, 4, P], F32, at=osb_at)]
        qtC = place("qtC", [P, KD, T], F32, at=arena)
        kC = place("kC", [P, T], F32, at=arena + 17408)
        kdup = place("kdup", [P, CKV, KEYS_C], F32, at=arena + 19584)
        vTC = place("vTC", [P, T], F32, at=arena + 24960)
        vC = place("vC", [P, 5, P], F32, at=arena + 27136)
        vC_cache = place("vC_cache", [P, P], F32, at=arena + 29696)
        ropeC = place("ropeC", [P, 4, T], F32, at=arena + 30208)
        swapC = place("swapC", [P, P], F32, at=arena + 38912)
        probsC = place("probsC", [P, 4, 512], F32, at=arena + 39424)
        probsTC = place("probsTC", [P, 2, 512], F32, at=arena + 47616)
        identC = place("identC", [P, P], F32R, at=arena + 52224)
        maskC = place("maskC", [P, 2 * P], F32R, at=arena + 52736)
        mask_rawC = place("mask_rawC", [P, 2 * P], F32, at=arena + 53760)
        osbC = [place("osbC%d" % i, [P, 4, P], F32, at=arena + 55296 + 2048 * i) for i in range(4)]
        osb = {"mla": osbA, "band": osbB, "swa": osbC}
        neg_sink = place("neg_sink", [P, CH + 4], F32, at=arena + 51712)
        sink = place("sink", [P, CH + 4], F32, at=arena + 51808)

        psum = ctx.enter_context(nc.psum_tensor("psum", [P, 8, 512], F32))

        def sem(name):
            return ctx.enter_context(nc.semaphore(name))

        gains_in = sem("gains_in")
        consts_in = sem("consts_in")
        x_in = [sem("x_inA"), sem("x_inB")]
        raw_in = [sem("raw_in0"), sem("raw_in1")]
        w_hi_done = sem("w_hi_done")
        w_lo_done = sem("w_lo_done")
        gains_ready = sem("gains_ready")
        std_ready = sem("std_ready")
        x_ready = sem("x_ready")
        xsq_ready = sem("xsq_ready")
        xhi_ready = sem("xhi_ready")
        xlo_ready = sem("xlo_ready")
        prestat = sem("prestat")
        proj_ready = sem("proj_ready")
        proj_read = sem("proj_read")
        gate_scaled = sem("gate_scaled")
        silu_done = sem("silu_done")
        h_ready = sem("h_ready")
        hhi_ready = sem("hhi_ready")
        hlo_ready = sem("hlo_ready")
        y_ready = sem("y_ready")
        ysq_ready = sem("ysq_ready")
        poststat = sem("poststat")
        dve_step = sem("dve_step")
        even_in = sem("even_in")
        pad_zero = sem("pad_zero")
        lat_sq = sem("lat_sq")
        lat_stat = sem("lat_stat")
        lat_std = sem("lat_std")
        lat_norm = sem("lat_norm")
        lat_hi = sem("lat_hi")
        lat_lo = sem("lat_lo")
        q_raw = sem("q_raw")
        q_copied = sem("q_copied")
        swapped = sem("swapped")
        roped = sem("roped")
        k_ready = sem("k_ready")
        k_copied = sem("k_copied")
        v_ready = sem("v_ready")
        v_copied = sem("v_copied")
        kpe_spread = sem("kpe_spread")
        band_in = sem("band_in")
        band_prep = sem("band_prep")
        rel_in = sem("rel_in")
        rel_shifted = sem("rel_shifted")
        mask_in = sem("mask_in")
        mask_ready = sem("mask_ready")
        band_act = sem("band_act")
        band_dve = sem("band_dve")
        odd_in = sem("odd_in")
        k_doubled = sem("k_doubled")
        c_roped = sem("c_roped")
        c_swapped = sem("c_swapped")
        vc_turned = sem("vc_turned")
        vc_copied = sem("vc_copied")
        sinks_ready = sem("sinks_ready")
        s_ready = sem("s_ready")
        max_ready = sem("max_ready")
        exp_done = sem("exp_done")
        o_scaled = sem("o_scaled")
        o_turned = sem("o_turned")
        pt_turned = sem("pt_turned")
        pt_ready = sem("pt_ready")
        pv_done = sem("pv_done")
        o_hi = sem("o_hi")
        o_lo = sem("o_lo")
        stored = sem("stored")
        latents_stored = sem("latents_stored")
        y_stored = sem("y_stored")

        block = ctx.enter_context(nc.Block())

        def slot(g, u):
            return 2 * (g % 2) + u

        def y_of(s):
            return y_ffn if SUBS[s] == "ffn" else y_mix

        def pre_gain(c):
            return 6 * (c // 3) + 2 * (c % 3)

        def ffn_no(s):
            return sum(k == "ffn" for k in SUBS[:s])

        def wait_group_used(eng, g):
            s = max(i for i in range(len(SUBS)) if G0[i] <= g)
            kind, j = SUBS[s], g - G0[s]
            if j < IN_STEPS[kind]:
                eng.wait_ge(proj_ready, P0[s] + max(2 * j + 2, 3))
            elif kind == "even" and j == 8:
                eng.wait_ge(q_raw, 2 * NH)
            elif kind == "even" and j == 9:
                eng.wait_ge(v_ready, 7)
            else:
                m = j - IN_STEPS[kind] - MID_GROUPS[kind]
                eng.wait_ge(y_ready, out_event(s, m if kind == "ffn" else 2 * m + 1, 1) + 1)

        def act_split(act, g, par, tiles, used=None):
            for u in range(2):
                act.wait_ge(raw_in[u], 16 * (g + 1))
                if u == 0 and used is not None:
                    used(act)
                n = tiles[u] * P
                nc.scalar.activation(w_hi[:, 2 * par + u, 0:n], w_raw[:, u, 0:n], ACT.Copy).then_inc(w_hi_done, 1)

        def dve_split(dve, g, par, tiles):
            for u in range(2):
                dve.wait_ge(w_hi_done, 2 * g + u + 1)
                n = tiles[u] * P
                nc.vector.tensor_tensor(w_lo[:, 2 * par + u, 0:n], w_raw[:, u, 0:n],
                                        w_hi[:, 2 * par + u, 0:n].bitcast(F32), ALU.subtract).then_inc(w_lo_done, 1)

        def split_group(eng, which, g):
            if g >= G0[-1]:
                return
            if which == "act":
                act_split(eng, g, g % 2, unit_tiles(g), (lambda e: wait_group_used(e, g - 2)) if g >= 2 else None)
            else:
                dve_split(eng, g, g % 2, unit_tiles(g))

        @block.sync
        def _(sp):
            sp.dma_start(gains[:], ins["gains"]).then_inc(gains_in, 16)
            sp.dma_start(x[:, :, HALF[0]], ins["x"][:, :, HALF[0]]).then_inc(x_in[0], 16)
            for u in range(2):
                sp.dma_start(w_raw[:, u, 0:D], ins["w_gate_up"][0, 0, u]).then_inc(raw_in[u], 16)
            sp.dma_start(ones[:], ins["ones"]).then_inc(consts_in, 16)
            sp.dma_start(x[:, :, HALF[1]], ins["x"][:, :, HALF[1]]).then_inc(x_in[1], 16)
            sp.dma_start(ident[:], ins["ident"]).then_inc(consts_in, 16)
            sp.dma_start(lat_gains[:], ins["lat_gains"]).then_inc(consts_in, 16)

            def load(g, u, source, n):
                sp.wait_ge(w_lo_done, 2 * (g - 1) + u + 1)
                sp.dma_start(w_raw[:, u, 0:n], source).then_inc(raw_in[u], 16)

            for s, kind in enumerate(SUBS):
                n = ffn_no(s)
                if kind == "ffn":
                    with sp.Fori(1 if s == 0 else 0, KF) as f:
                        for u in range(2):
                            load(f + G0[s], u, ins["w_gate_up"][n, f, u], D)
                    with sp.Fori(0, KD) as m:
                        for u in range(2):
                            load(m + (G0[s] + KF), u, ins["w_down"][n, m, u], UW)
                else:
                    names = ["even_in"] * 8 + ["mla_up"] * 2 + ["even_out"] * 4 if kind == "even" else \
                        ["odd_in"] * 5 + ["odd_out"] * 4
                    for j, name in enumerate(names):
                        for u in range(2):
                            cols = unit_tiles(G0[s] + j)[u] * P
                            if name == "mla_up":
                                source = ins[("mla_uq", "mla_ukv")[j - 8]]
                                source = source[u] if j == 8 else source[:, 0:D] if u == 0 else source[:, D:D + 512]
                            else:
                                source = ins[name][names[:j].count(name), u]
                            load(G0[s] + j, u, source, cols)
            c = len(SUBS)
            for H in range(2):
                for k in range(KD):
                    sp.wait_ge(x_ready, 16 * (c - 1) + 8 * H + k + 1)
                    sp.dma_start(outs["y"][:, k, HALF[H]], x[:, k, HALF[H]]).then_inc(y_stored, 16)
            sp.wait_ge(y_stored, 16 * 2 * KD)

        def mm3(out, s_hi, s_lo, m_hi, m_lo, first, last):
            nc.tensor.matmul(out, s_hi, m_hi, start=first, stop=False)
            nc.tensor.matmul(out, s_hi, m_lo, start=False, stop=False)
            return nc.tensor.matmul(out, s_lo, m_hi, start=False, stop=last)

        @block.tensor
        def _(pe):
            def in_half(s, g, par, event, H, bank, c=None):
                for u in range(2):
                    pe.wait_ge(w_lo_done, 2 * g + u + 1)
                    for k in range(KD):
                        if c is not None and u == 0:
                            pe.wait_ge(xlo_ready, 16 * c + 8 * H + k + 1)
                        mm = mm3(psum[:, bank + u, 0:TH],
                                 w_hi[:, 2 * par + u, k * P:(k + 1) * P], w_lo[:, 2 * par + u, k * P:(k + 1) * P],
                                 xhi[:, k, HALF[H]], xlo[:, k, HALF[H]], k == 0, k == KD - 1)
                        if c is not None and u == 0:
                            pre_square(c, H, k)
                            if c > 0 and H == 0 and k == 2:
                                post_square(c - 1, KD - 1, 1)
                mm.then_inc(proj_ready, 1)

            def pre_square(c, H, k):
                pe.wait_ge(xsq_ready, 16 * c + 8 * H + k + 1)
                if k == 0 and c > 0:
                    pe.wait_ge(std_ready, std_event(c, True, H) + 1)
                nc.tensor.matmul(psum[:, 6 + H, 0:TH], ones[:], squares[:, k, HALF[H]],
                                 start=k == 0, stop=k == KD - 1).then_inc(prestat, 1)

            def first_steps(s):
                g, c = G0[s], s
                if s > 0:
                    pe.wait_ge(ysq_ready, out_event(s - 1, KD - 2, 1) + 1)
                in_half(s, g, g % 2, P0[s], 0, 0, c)
                if s > 0:
                    pe.wait_ge(std_ready, std_event(c, True, 1) + 1)
                in_half(s, g + 1, (g + 1) % 2, P0[s] + 1, 0, 4)
                if s > 0:
                    pe.wait_ge(ysq_ready, 16 * s)
                in_half(s, g, g % 2, P0[s] + 2, 1, 2, c)
                pe.wait_ge(std_ready, std_event(c, False, 1) + 1)
                in_half(s, g + 1, (g + 1) % 2, P0[s] + 3, 1, 6)

            def out_half(s, g, par, e, H, first, mid, part=None):
                ffn = SUBS[s] == "ffn"
                tiles = OUT_TILES[SUBS[s]]
                a_hi, a_lo = (h_hi, h_lo) if ffn else (xhi, xlo)
                for k in part or range(tiles):
                    if not ffn and first:
                        pe.wait_ge(o_lo, heads_ready(SUBS[s], k, H))
                    if ffn and first and k in (0, KF - 1):
                        pe.wait_ge(hlo_ready, 2 * KF * ffn_no(s) + 2 * (KF - 1) + (H + 1 if k else 0))
                    u, j = (k // DU, k % DU) if ffn else (e, k)
                    if j == 0:
                        pe.wait_ge(w_lo_done, 2 * g + u + 1)
                    w = slice(j * P, (j + 1) * P)
                    mm = mm3(psum[:, 2 * e + H, 0:TH], w_hi[:, 2 * par + u, w], w_lo[:, 2 * par + u, w],
                             a_hi[:, k, HALF[H]], a_lo[:, k, HALF[H]], k == 0, k == tiles - 1)
                    if k == tiles // 2 and mid is not None:
                        mid()
                if k == tiles - 1:
                    mm.then_inc(y_ready, 1)

            def post_square(s, m, H, event=None, first=False):
                pe.wait_ge(ysq_ready, (out_event(s, m, H) if event is None else event) + 1)
                nc.tensor.matmul(psum[:, 4 + H, 0:TH], ones[:], scratch[:, 2 * H + m % 2, :],
                                 start=first, stop=True, skip_group_check=True).then_inc(poststat, 1)

            def ffn_pair(s, i, first=False):
                g = G0[s] + KF
                for n, (e, H) in enumerate([(0, 0), (1, 0), (0, 1), (1, 1)]):
                    event = i * 4 + (16 * s + n)
                    if not first:
                        pe.wait_ge(ysq_ready, event - 3)
                    pe_, pH = [(1, 1), (0, 0), (1, 0), (0, 1)][n]
                    mid = None if first and n == 0 else \
                        (lambda: post_square(s, pe_, pH, event - 1, first=first and n in (1, 3)))
                    out_half(s, i * 2 + (g + e), (g + e) % 2, e, H, first and e == 0, mid)

            def out_early(s, n, name):
                if n == len(ATT[name][0]) + 4:
                    out_half(s, G0[s + 1] - 4, G0[s + 1] % 2, 0, 0, True, None, EARLY)

            def out_projection(s):
                if SUBS[s] == "ffn":
                    ffn_pair(s, 0, first=True)
                    with pe.Fori(1, KD // 2) as i:
                        ffn_pair(s, i)
                    return
                g = G0[s + 1] - 4
                before = None
                for m, H in out_order(SUBS[s]):
                    if before is None:
                        out_half(s, g, g % 2, 0, 0, True, None, EARLY_REST)
                        before = (m, H)
                        continue
                    if m >= 2:
                        pe.wait_ge(ysq_ready, out_event(s, m - 2, H) + 1)
                    mid = None if before is None else \
                        (lambda: post_square(s, *before, first=before[0] == 0))
                    out_half(s, g + m // 2, (g + m // 2) % 2, m % 2, H, m == 0, mid)
                    before = (m, H)

            def attention(name, between=None):
                items, done = ATT[name]
                base, obase = A0[name], O0[name]
                N = len(items)
                probs, probsT = (probsC, probsTC) if name == "swa" else (probsE, probsTE)

                unit = identC if name == "swa" else identE

                def add(out, what):
                    return nc.tensor.matmul(out, unit[:], what, start=False, stop=True, skip_group_check=True)

                def scores(n):
                    it, bank = items[n], n % 3
                    if name == "swa" and n in (8, 16):
                        pe.wait_ge(c_roped, n + 2)
                    if n >= 3:
                        pe.wait_ge(exp_done, base + n - 2)
                    if it["kind"] == "prompt":
                        i, w = it["i"], it["width"]
                        q = slice(P * i, P * (i + 1))
                        if name == "mla":
                            nc.tensor.matmul(psum[:, bank, 0:w], qtA[:, it["h"], q], ktA[:, it["h"], 0:w],
                                             start=True, stop=True)
                            mm = add(psum[:, bank, w - P:w], maskE[:, P:2 * P])
                        elif name == "band":
                            h, near = it["h"], min(w, 2 * P)
                            r = slice(64 * (h % 2), 64 * (h % 2) + 64)
                            nc.tensor.matmul(psum[:, bank, 0:w], qkvb[r, h // 2, q], qkvb[r, 4 + h // 2, 0:w],
                                             start=True, stop=True)
                            add(psum[:, bank, w - near:w], rel_hi[:, h, 2 * P - near:2 * P])
                            mm = add(psum[:, bank, w - near:w], rel_lo[:, h, 2 * P - near:2 * P])
                        else:
                            lo = P * max(i - 1, 0)
                            for d in range(2):
                                h = it["h"] + 2 * d
                                r = slice(64 * (h % 2), 64 * (h % 2) + 64)
                                nc.tensor.matmul(psum[:, bank, d * w:(d + 1) * w], qtC[r, h // 2, q],
                                                 kdup[r, h // 8, lo:lo + w], start=True, stop=True)
                                mm = add(psum[:, bank, d * w:(d + 1) * w], maskC[:, 2 * P - w:2 * P])
                    else:
                        if name == "band":
                            nc.tensor.matmul(psum[:, bank, 0:SK], unit[:], relS_hi[:, it["h"] // 4, :],
                                             start=True, stop=True)
                            add(psum[:, bank, 0:SK], relS_lo[:, it["h"] // 4, :])
                        for d in range(4):
                            h = it["h"] + d
                            rows = slice(32 * d, 32 * d + 32)
                            r = slice(64 * (h % 2), 64 * (h % 2) + 64)
                            if name == "mla":
                                mm = nc.tensor.matmul(psum[rows, bank, 0:SK], qtA[:, h, SEQ:T],
                                                      ktA[:, h, SEQ:KEYS_A], start=True, stop=True)
                            elif name == "band":
                                nc.tensor.matmul(psum[rows, bank, 0:DEC], qkvb[r, h // 2, SEQ:T],
                                                 qkvb[r, 4 + h // 2, SEQ:T], start=False, stop=True,
                                                 skip_group_check=True)
                                mm = nc.tensor.matmul(psum[rows, bank, DEC:SK], qkvb[r, h // 2, SEQ:T],
                                                      kB_cache[r, h // 2, :], start=False, stop=True,
                                                      skip_group_check=True)
                            else:
                                mm = nc.tensor.matmul(psum[rows, bank, 0:DEC + P], qtC[r, h // 2, SEQ:T],
                                                      kdup[r, h // 8, SEQ:KEYS_C], start=True, stop=True)
                    mm.then_inc(s_ready, 1)

                def turn(n):
                    pe.wait_ge(exp_done, base + n + 1)
                    if n >= 2:
                        pe.wait_ge(pt_ready, base + n - 1)
                    for j, (col, kw) in enumerate(items[n]["pieces"]):
                        mm = nc.tensor.transpose(psum[0:kw, 3 + n % 2, j * P:(j + 1) * P],
                                                 probs[:, n % 4, col:col + kw], ident[:])
                    mm.then_inc(pt_turned, 1)

                def values(n):
                    it, bank = items[n], 5 + n % 2
                    pe.wait_ge(pt_ready, base + n + 1)
                    if n >= 2:
                        pe.wait_ge(o_scaled, base + n - 1)
                    if it["kind"] == "prompt":
                        heads = 2 if name == "swa" else 1
                        per = len(it["pieces"]) // heads
                        for d in range(heads):
                            h = it["h"] + 2 * d
                            for j in range(per):
                                if name == "mla":
                                    v = vA[:, j, h * HD:(h + 1) * HD]
                                elif name == "band":
                                    v = vB[:, j, h * HD:(h + 1) * HD]
                                else:
                                    v = vC[:, max(it["i"] - 1, 0) + j, (h // 8) * HD:(h // 8 + 1) * HD]
                                p = (d * per + j) * P
                                mm = nc.tensor.matmul(psum[:, bank, HD * d:HD * (d + 1)], probsT[:, n % 2, p:p + P], v,
                                                      start=j == 0, stop=j == per - 1)
                    else:
                        for d in range(4):
                            h, pieces = it["h"] + d, it["pieces"]
                            for j, (_, kw) in enumerate(pieces):
                                if name == "mla":
                                    v = vA[0:kw, 4 + j, h * HD:(h + 1) * HD]
                                elif name == "band":
                                    v = (vB_cache[:, j, h * HD:(h + 1) * HD] if kw == P
                                         else vB[0:kw, 4, h * HD:(h + 1) * HD])
                                else:
                                    c0 = (h // 8) * HD
                                    v = vC_cache[:, c0:c0 + HD] if kw == P else vC[0:kw, 4, c0:c0 + HD]
                                mm = nc.tensor.matmul(psum[32 * d:32 * d + 32, bank, 0:HD],
                                                      probsT[0:kw, n % 2, j * P + 32 * d:j * P + 32 * d + 32], v,
                                                      start=j == 0, stop=j == len(pieces) - 1)
                    mm.then_inc(pv_done, 1)

                def turn_outputs(k):
                    last, _, blocks, _ = done[k]
                    pe.wait_ge(o_scaled, base + last + 1)
                    if obase + k:
                        pe.wait_ge(o_lo, obase + k)
                    for b in range(blocks):
                        mm = nc.tensor.transpose(psum[:, 7, b * P:(b + 1) * P], osb[name][k % len(osb[name])][:, b, :], ident[:])
                    mm.then_inc(o_turned, 1)

                k = 0
                for n in range(N + 6):
                    if n < N:
                        scores(n)
                    if between:
                        between(n)
                    if 3 <= n < N + 3:
                        turn(n - 3)
                    if 4 <= n < N + 4:
                        values(n - 4)
                    if k < len(done) and done[k][0] + 6 <= n:
                        turn_outputs(k)
                        k += 1

            def even_middle(s):
                g = G0[s] + 8
                pe.wait_ge(even_in, 16 * 5)

                def query(q):
                    h, H = q // 2, q % 2
                    u, hh = h // 4, h % 4
                    if q == 0:
                        pe.wait_ge(lat_lo, 6)
                        pe.wait_ge(proj_read, P0[s] + 16)
                    if q % 8 == 0:
                        pe.wait_ge(w_lo_done, 2 * g + u + 1)
                    if q >= 4:
                        pe.wait_ge(q_copied, q - 3)
                    for k in range(2):
                        w = slice(k * 4 * QK + hh * QK, k * 4 * QK + (hh + 1) * QK)
                        mm = mm3(psum[0:QK, q % 4, 0:TH], w_hi[:, slot(g, u), w], w_lo[:, slot(g, u), w],
                                 cqn_hi[:, k, HALF[H]], cqn_lo[:, k, HALF[H]], k == 0, k == 1)
                    mm.then_inc(q_raw, 1)

                def swap(j):
                    if j < 2:
                        raw = kpe_raw[0:QK, HALF[j]]
                        pe.wait_ge(lat_std, 2)
                    else:
                        pe.wait_ge(q_copied, j - 1)
                        raw = qtA[:, (j - 2) // 2, HALF[j % 2]]
                    if j >= 4:
                        pe.wait_ge(roped, j - 3)
                    nc.tensor.matmul(psum[0:QK, 4 + j % 4, 0:TH], swapA[:], raw,
                                     start=True, stop=True).then_inc(swapped, 1)

                swap(0)
                swap(1)
                for q in range(2 * NH):
                    query(q)
                    if q >= 1:
                        swap(q + 1)
                swap(2 * NH + 1)
                pe.wait_ge(lat_lo, 7)
                pe.wait_ge(pad_zero, 2)
                pe.wait_ge(w_lo_done, 2 * (g + 1) + 1)
                for j in range(2 * NH):
                    h, c = j // 2, j % 2
                    cols = slice(c * (KEYS_A // 2), (c + 1) * (KEYS_A // 2))
                    if j < 4:
                        pe.wait_ge(q_copied, 2 * NH)
                    else:
                        pe.wait_ge(k_copied, j - 3)
                    w = slice(h * P, (h + 1) * P)
                    mm3(psum[:, j % 4, 0:KEYS_A // 2], w_hi[:, slot(g + 1, 0), w], w_lo[:, slot(g + 1, 0), w],
                        ckv_hi[:, cols], ckv_lo[:, cols], True, True).then_inc(k_ready, 1)
                pe.wait_ge(w_lo_done, 2 * (g + 1) + 2)
                pe.wait_ge(roped, 2 * NH + 2)
                for v in range(7):
                    cols = slice(v * P, (v + 1) * P)
                    if v >= 4:
                        pe.wait_ge(v_copied, v - 3)
                    mm3(psum[:, 4 + v % 4, :], ckv_hi[:, cols], ckv_lo[:, cols],
                        w_hi[:, slot(g + 1, 1), 0:512], w_lo[:, slot(g + 1, 1), 0:512], True, True).then_inc(v_ready, 1)
                pe.wait_ge(k_copied, 2 * NH)
                pe.wait_ge(v_copied, 7)
                pe.wait_ge(kpe_spread, 16)
                pe.wait_ge(mask_ready, 2)

            def band_ready(s):
                def job(j):
                    if j == 5:
                        pe.wait_ge(rel_shifted, 10)
                        pe.wait_ge(o_lo, O0["band"])
                    if j >= 8:
                        pe.wait_ge(band_act if j % 2 == 0 else band_dve, (j - 8) // 2 + 1)
                    if j < 5:
                        n = P if j < 4 else DEC
                        for v in range(4):
                            mm = nc.tensor.transpose(psum[0:n, j, v * P:(v + 1) * P],
                                                     qkvb[:, 8 + v, j * P:j * P + n], ident[:])
                    elif j < 9:
                        nc.tensor.matmul(psum[:, j % 8, :], flips[:, 0, :],
                                         hankel[:, 2 * (j - 5):2 * (j - 4), :].rearrange("p h k -> p (h k)"),
                                         start=True, stop=True)
                        for h in range(2):
                            mm = nc.tensor.matmul(psum[:, j % 8, 2 * P * h:2 * P * (h + 1)], identE[:], maskE[:],
                                                  start=False, stop=True, skip_group_check=True)
                    else:
                        mm = nc.tensor.matmul(psum[:, j % 8, 0:SK], flips[:, 1, :], hankelS[:, j - 9, :],
                                              start=True, stop=True)
                    mm.then_inc(band_prep, 1)

                pe.wait_ge(exp_done, A0["band"])
                pe.wait_ge(pt_ready, A0["band"])
                for j in range(11):
                    job(j)
                pe.wait_ge(band_act, 9)
                pe.wait_ge(band_dve, 8)
                pe.wait_ge(band_in, 16 * 2)

            pe.wait_ge(consts_in, 16 * 3)
            for s, kind in enumerate(SUBS):
                first_steps(s)
                g = G0[s]
                if kind == "ffn":
                    with pe.Fori(1, KF // 2) as i:
                        for e in range(2):
                            for H in range(2):
                                pe.wait_ge(proj_read, i * 4 + (P0[s] + (1, 3, 3, 4)[2 * e + H] - 4))
                                in_half(s, i * 2 + (g + e), (g + e) % 2, None, H, 4 * e + 2 * H)
                elif kind == "even":
                    for f in range(2, 8):
                        for H in range(2):
                            pe.wait_ge(proj_read, P0[s] + ((1, 3)[H] if f == 2 else 2 * f + H - 1))
                            in_half(s, g + f, (g + f) % 2, None, H, 2 * H)
                        if f == 4:
                            pe.wait_ge(proj_read, P0[s] + 4)
                            for H in range(2):
                                pe.wait_ge(lat_sq, 3 * H + 3)
                                for t in range(2):
                                    nc.tensor.matmul(psum[:, 4 + H, 0:TH], ones[:], scratch[:, 2 * H + t, :],
                                                     start=t == 0, stop=t == 1)
                                nc.tensor.matmul(psum[:, 6 + H, 0:TH], ones[:], lat_rstd[:, 1, HALF[H]],
                                                 start=True, stop=True).then_inc(lat_stat, 1)
                    even_middle(s)
                    attention("mla")
                    band_ready(s)
                    attention("band", lambda n: out_early(s, n, "band"))
                else:
                    def swap_c(j):
                        if j < 2:
                            raw = kC[:, HALF[j]]
                        else:
                            raw = qtC[:, j // 2 - 1, HALF[j % 2]]
                        if j >= 4:
                            pe.wait_ge(c_roped, j - 3 if j < 10 else j)
                        nc.tensor.matmul(psum[:, 4 + j % 4 if j < 10 else 7, 0:TH], swapC[:], raw,
                                         start=True, stop=True).then_inc(c_swapped, 1)

                    pe.wait_ge(odd_in, 16 * 7)
                    for f in range(2, 5):
                        for H in range(2):
                            pe.wait_ge(proj_read, P0[s] + ((1, 3)[H] if f == 2 else 2 * f + H - 1))
                            in_half(s, g + f, (g + f) % 2, None, H, 2 * H)
                            if f >= 3:
                                if f == 3 and H == 0:
                                    pe.wait_ge(proj_read, P0[s] + 4)
                                    swap_c(0)
                                    swap_c(1)
                                    for t in range(4):
                                        mm = nc.tensor.transpose(psum[:, 6, t * P:(t + 1) * P],
                                                                 vTC[:, t * P:(t + 1) * P], ident[:])
                                    mm.then_inc(vc_turned, 1)
                                    nc.tensor.transpose(psum[0:DEC, 7, 0:P], vTC[:, SEQ:T],
                                                        ident[:]).then_inc(vc_turned, 1)
                                if f == 3 and H == 1:
                                    pe.wait_ge(vc_copied, 2)
                                    for j in range(2, 6):
                                        swap_c(j)
                                if f == 4:
                                    if H == 0:
                                        pe.wait_ge(proj_read, P0[s] + 6)
                                    for j in (6 + 2 * H, 7 + 2 * H):
                                        swap_c(j)
                    pe.wait_ge(proj_read, P0[s] + 10)
                    pe.wait_ge(c_roped, 6)
                    pe.wait_ge(k_doubled, 16 * 4)
                    pe.wait_ge(mask_ready, 4)

                    def between(n):
                        if 1 <= n <= 8:
                            swap_c(9 + n)
                        out_early(s, n, "swa")

                    attention("swa", between)
                out_projection(s)
            post_square(len(SUBS) - 1, KD - 1, 1)

        def attention_act(act, name):
            items, done = ATT[name]
            base, obase = A0[name], O0[name]
            N = len(items)
            probs, probsT = (probsC, probsTC) if name == "swa" else (probsE, probsTE)

            def exponentials(n):
                it, w, part = items[n], items[n]["width"], soft[:, n % 8, :]
                act.wait_ge(max_ready, base + n + 1)
                if n >= 4:
                    act.wait_ge(pt_turned, base + n - 3)
                heads = 2 if name == "swa" and it["kind"] == "prompt" else 1
                if name == "swa":
                    nc.scalar.activation(part[:, 4:4 + heads], part[:, 4:4 + heads], ACT.Exp)
                for d in range(heads):
                    e = nc.scalar.activation(probs[:, n % 4, d * w:(d + 1) * w], psum[:, n % 3, d * w:(d + 1) * w],
                                             ACT.Exp, bias=part[:, d:d + 1], accum_out=part[:, 2 + d:3 + d])
                e.then_inc(exp_done, 1)

            def copy_turned(n):
                pieces = items[n]["pieces"]
                act.wait_ge(pt_turned, base + n + 1)
                if n >= 2:
                    act.wait_ge(pv_done, base + n - 1)
                full = sum(kw == P for _, kw in pieces) * P
                e = nc.scalar.activation(probsT[:, n % 2, 0:full], psum[:, 3 + n % 2, 0:full], ACT.Copy)
                if full < len(pieces) * P:
                    e = nc.scalar.activation(probsT[0:32, n % 2, full:full + P], psum[0:32, 3 + n % 2, full:full + P],
                                             ACT.Copy)
                e.then_inc(pt_ready, 1)

            def head_outputs(k):
                act.wait_ge(o_turned, obase + k + 1)
                for out, src in output_views(*done[k], xhi):
                    e = nc.scalar.activation(out, src, ACT.Copy)
                e.then_inc(o_hi, 1)

            k = 0
            for n in range(N + 7):
                if 3 <= n < N + 3:
                    copy_turned(n - 3)
                if n < N:
                    exponentials(n)
                if k < len(done) and done[k][0] + 7 <= n:
                    head_outputs(k)
                    k += 1

        def band_result(j):
            if j < 5:
                n = P if j < 4 else DEC
                return vB[0:n, j, :], None, psum[0:n, j, :]
            if j < 9:
                h = slice(2 * (j - 5), 2 * (j - 4))
                return (rel_hi[:, h, :].rearrange("p h k -> p (h k)"), rel_lo[:, h, :].rearrange("p h k -> p (h k)"),
                        psum[:, j % 8, :])
            return relS_hi[:, j - 9, :], relS_lo[:, j - 9, :], psum[:, j % 8, 0:SK]

        def output_views(last, tile, blocks, kind, to):
            if kind == "prompt":
                return [(to[:, tile, 0:SEQ], psum[:, 7, :])]
            tiles = psum[:, 7, 0:blocks * P].rearrange("p (t c) -> p t c", c=2 * DEC)
            return [(to[64 * e:64 * e + 64, tile:tile + 2 * blocks, SEQ:T],
                     tiles[64 * e:64 * e + 64, :, DEC * e:DEC * (e + 1)]) for e in range(2)]

        @block.scalar
        def _(act):
            def post_std(c, H):
                act.wait_ge(poststat, out_event(c - 1, KD - 1, H) + 1)
                nc.scalar.activation(rstd[:, HALF[H]], psum[:, 4 + H, 0:TH], ACT.Sqrt, bias=eps[:],
                                     scale=1.0 / D).then_inc(std_ready, 1)

            def pre_std(c, H):
                act.wait_ge(prestat, 16 * c + 8 * H + KD)
                nc.scalar.activation(rstd[:, HALF[H]], psum[:, 6 + H, 0:TH], ACT.Sqrt, bias=eps[:],
                                     scale=1.0 / D).then_inc(std_ready, 1)

            def tile(c, H, k):
                if c == 0:
                    if k == 0:
                        act.wait_ge(x_in[H], 16)
                else:
                    act.wait_ge(x_ready, 16 * (c - 1) + 8 * H + k + 1)
                nc.scalar.activation(squares[:, k, HALF[H]], x[:, k, HALF[H]], ACT.Square).then_inc(xsq_ready, 1)
                nc.scalar.activation(xhi[:, k, HALF[H]], x[:, k, HALF[H]], ACT.Copy,
                                     scale=gains[:, pre_gain(c), k:k + 1]).then_inc(xhi_ready, 1)

            def boundary(c):
                g = G0[c]
                if c == 0:
                    for k in range(KD):
                        tile(c, 0, k)
                    split_group(act, "act", 0)
                    for k in range(KD):
                        tile(c, 1, k)
                    split_group(act, "act", 1)
                    pre_std(c, 0)
                    pre_std(c, 1)
                    return
                s = c - 1
                post_std(c, 0)
                takes = {3: [6], 7: [7]} if SUBS[s] == "ffn" else {-1: [4], 1: [5], 3: [6], 5: [7]}
                split_at = 3 if SUBS[s] == "ffn" else 1
                for k in range(-1, KD):
                    if k >= 0 and c < len(SUBS):
                        tile(c, 0, k)
                    for m in takes.get(k, []):
                        out_result(s, out_event(s, m, 1), m, m % 2, 1)
                    if k == split_at:
                        split_group(act, "act", g)
                post_std(c, 1)
                if c == len(SUBS):
                    return
                split_group(act, "act", g + 1)
                pre_std(c, 0)
                for k in range(KD):
                    tile(c, 1, k)
                pre_std(c, 1)

            def gate_half(n, f, H):
                e = f * 2 + (2 * KF * n + H)
                act.wait_ge(gate_scaled, e + 1)
                nc.scalar.activation(scratch[:, 2 * H, :], scratch[:, 2 * H, :], ACT.Silu).then_inc(silu_done, 1)
                act.wait_ge(h_ready, e + 1)
                nc.scalar.activation(h_hi[:, f, HALF[H]], scratch[:, 2 * H, :], ACT.Copy).then_inc(hhi_ready, 1)

            def gate_first(n, f, H):
                e = 2 * KF * n + 2 * H + f
                act.wait_ge(gate_scaled, e + 1)
                nc.scalar.activation(scratch[:, 2 * H, :], scratch[:, 2 * H, :], ACT.Silu).then_inc(silu_done, 1)
                act.wait_ge(h_ready, e + 1)
                nc.scalar.activation(h_hi[:, f, HALF[H]], scratch[:, 2 * H, :], ACT.Copy).then_inc(hhi_ready, 1)

            def out_result(s, event, m, e, H, first=False):
                act.wait_ge(y_ready, event + 1)
                nc.scalar.activation(y_of(s)[:, m, HALF[H]], psum[:, 2 * e + H, 0:TH], ACT.Copy)
                if not first:
                    act.wait_ge(poststat, event - 3 if not isinstance(event, int) else out_event(s, m - 2, H) + 1)
                nc.scalar.activation(scratch[:, 2 * H + e, :], psum[:, 2 * e + H, 0:TH],
                                     ACT.Square).then_inc(ysq_ready, 1)

            act.wait_ge(gains_ready, 7)
            for s, kind in enumerate(SUBS):
                g, n = G0[s], ffn_no(s)
                boundary(s)
                if kind == "ffn":
                    split_group(act, "act", g + 2)
                    gate_first(n, 0, 0)
                    gate_first(n, 1, 0)
                    gate_first(n, 0, 1)
                    gate_first(n, 1, 1)
                    with act.Fori(1, KF // 2 - 1) as i:
                        for e in range(2):
                            f = i * 2 + e
                            act_split(act, f + (g + 1), (g + e + 1) % 2, (KD, KD),
                                      lambda eng: eng.wait_ge(proj_ready, f * 2 + P0[s]))
                            for H in range(2):
                                gate_half(n, f, H)
                    for f in (KF - 2, KF - 1):
                        split_group(act, "act", g + f + 1)
                        for H in range(2):
                            gate_half(n, f, H)
                    split_group(act, "act", g + KF + 1)
                    for e, H in ((0, 0), (1, 0), (0, 1)):
                        out_result(s, out_event(s, e, H), e, e, H, first=True)
                    split_group(act, "act", g + KF + 2)
                    out_result(s, out_event(s, 1, 1), 1, 1, 1, first=True)
                    with act.Fori(1, KD // 2 - 1) as i:
                        act_split(act, i * 2 + (g + KF + 1), (g + KF + 1) % 2, (DU, DU),
                                  lambda eng: eng.wait_ge(y_ready, i * 4 + 16 * s))
                        for n_, (e, H) in enumerate([(0, 0), (1, 0), (0, 1)]):
                            out_result(s, i * 4 + (16 * s + n_), i * 2 + e, e, H)
                        act_split(act, i * 2 + (g + KF + 2), (g + KF) % 2, (DU, DU),
                                  lambda eng: eng.wait_ge(y_ready, i * 4 + (16 * s + 3)))
                        out_result(s, i * 4 + (16 * s + 3), i * 2 + 1, 1, 1)
                    split_group(act, "act", g + KF + KD - 1)
                    for m in (KD - 2, KD - 1):
                        out_result(s, out_event(s, m, 0), m, m % 2, 0)
                    continue
                if kind == "even":
                    split_group(act, "act", g + 2)
                    for H in range(2):
                        act.wait_ge(proj_read, P0[s] + 2 + 2 * H)
                        for t in range(2):
                            nc.scalar.activation(scratch[:, 2 * H + t, :], cq[:, t, HALF[H]],
                                                 ACT.Square).then_inc(lat_sq, 1)
                        nc.scalar.activation(lat_rstd[:, 1, HALF[H]], ckv[:, HALF[H]], ACT.Square).then_inc(lat_sq, 1)
                    for f in (3, 4, 5):
                        split_group(act, "act", g + f)
                    for H in range(2):
                        act.wait_ge(lat_stat, H + 1)
                        nc.scalar.activation(lat_rstd[:, 0, HALF[H]], psum[:, 4 + H, 0:TH], ACT.Sqrt,
                                             bias=eps[:], scale=1.0 / 256)
                        nc.scalar.activation(lat_rstd[:, 1, HALF[H]], psum[:, 6 + H, 0:TH], ACT.Sqrt,
                                             bias=eps[:], scale=1.0 / 128).then_inc(lat_std, 1)
                    act.wait_ge(even_in, 16 * 5)
                    nc.scalar.activation(ckv_hi[:, T:KEYS_A], ckv_cache[:], ACT.Copy).then_inc(lat_hi, 1)
                    for H in range(2):
                        act.wait_ge(lat_norm, 3 * H + 3)
                        for t in range(2):
                            nc.scalar.activation(cqn_hi[:, t, HALF[H]], cq[:, t, HALF[H]], ACT.Copy).then_inc(lat_hi, 1)
                        nc.scalar.activation(ckv_hi[:, HALF[H]], ckv[:, HALF[H]], ACT.Copy).then_inc(lat_hi, 1)
                    for f in (6, 7, 8):
                        split_group(act, "act", g + f)
                    split_group(act, "act", g + 9)
                    for q in range(2 * NH):
                        act.wait_ge(q_raw, q + 1)
                        nc.scalar.activation(qtA[:, q // 2, HALF[q % 2]], psum[0:QK, q % 4, 0:TH], ACT.Copy,
                                             scale=A_SCALE).then_inc(q_copied, 1)
                    split_group(act, "act", g + 10)
                    for j in range(2 * NH):
                        act.wait_ge(k_ready, j + 1)
                        if j == 0:
                            act.wait_ge(lat_lo, 7)
                            act.wait_ge(roped, 2)
                            act.wait_ge(latents_stored, 16)
                        c = slice((j % 2) * (KEYS_A // 2), (j % 2 + 1) * (KEYS_A // 2))
                        nc.scalar.activation(ktA[0:NOPE, j // 2, c], psum[0:NOPE, j % 4, 0:KEYS_A // 2],
                                             ACT.Copy).then_inc(k_copied, 1)
                    act.wait_ge(roped, 2 * NH + 2)
                    nc.scalar.activation(identE[:], ident[:], ACT.Copy).then_inc(mask_ready, 1)
                    act.wait_ge(mask_in, 16)
                    nc.scalar.activation(maskE[:], mask_rawE[:], ACT.Copy).then_inc(mask_ready, 1)
                    attention_act(act, "mla")
                    for j in range(11):
                        if j % 2 and j < 5:
                            continue
                        act.wait_ge(band_prep, j + 1)
                        out, _, src = band_result(j)
                        nc.scalar.activation(out, src, ACT.Copy).then_inc(band_act, 1)
                    attention_act(act, "band")
                else:
                    for f in (2, 3, 4):
                        split_group(act, "act", g + f)
                    act.wait_ge(vc_turned, 1)
                    nc.scalar.activation(vC[:, 0:4, :].rearrange("p t c -> p (t c)"), psum[:, 6, :],
                                         ACT.Copy).then_inc(vc_copied, 1)
                    act.wait_ge(vc_turned, 2)
                    nc.scalar.activation(vC[0:DEC, 4, :], psum[0:DEC, 7, 0:P], ACT.Copy).then_inc(vc_copied, 1)
                    split_group(act, "act", g + 5)
                    act.wait_ge(odd_in, 16 * 7)
                    nc.scalar.activation(identC[:], ident[:], ACT.Copy).then_inc(mask_ready, 1)
                    nc.scalar.activation(maskC[:], mask_rawC[:], ACT.Copy).then_inc(mask_ready, 1)
                    attention_act(act, "swa")
                    act.wait_ge(stored, 16 * 4)
                og = G0[s + 1] - 4
                for n_, (m, H) in enumerate(out_order(kind)[:12]):
                    if n_ in (0, 4, 8):
                        split_group(act, "act", og + n_ // 4 + 1)
                    out_result(s, out_event(s, m, H), m, m % 2, H, first=m < 2)
            boundary(len(SUBS))

        @block.vector
        def _(dve):
            steps = [0]

            def own(ins):
                ins.then_inc(dve_step, 1)
                steps[0] += 1
                return steps[0]

            def own_wait(n):
                dve.wait_ge(dve_step, n)

            def reciprocal(c, post, H):
                dve.wait_ge(std_ready, std_event(c, post, H) + 1)
                own_wait(own(nc.vector.reciprocal(rstd[:, HALF[H]], rstd[:, HALF[H]])))

            def update(c, H, split_after=None):
                s = c - 1
                y = y_of(s)

                def scaled(k):
                    return own(nc.vector.scalar_tensor_tensor(
                        out=y[:, k, HALF[H]], in0=y[:, k, HALF[H]], scalar=post_gains[:, s, k:k + 1],
                        in1=rstd[:, HALF[H]], op0=ALU.mult, op1=ALU.mult))

                n = scaled(0)
                for k in range(KD):
                    n_next = scaled(k + 1) if k + 1 < KD else None
                    own_wait(n)
                    nc.vector.tensor_tensor(x[:, k, HALF[H]], x[:, k, HALF[H]], y[:, k, HALF[H]],
                                            ALU.add).then_inc(x_ready, 1)
                    n = n_next
                    if c < len(SUBS) and k >= 1:
                        low_part(c, H, k - 1)
                    if k == split_after:
                        split_group(dve, "dve", G0[c])
                if c < len(SUBS):
                    low_part(c, H, KD - 1)

            def boundary(c):
                if c == 0:
                    for k in range(KD):
                        low_part(c, 0, k)
                    split_group(dve, "dve", 0)
                    for k in range(KD):
                        low_part(c, 1, k)
                    split_group(dve, "dve", 1)
                else:
                    reciprocal(c, True, 0)
                    update(c, 0, 4 if SUBS[c - 1] == "ffn" else 2)
                    reciprocal(c, True, 1)
                    split_group(dve, "dve", G0[c] + 1)
                    update(c, 1)
                if c < len(SUBS):
                    reciprocal(c, False, 0)
                    reciprocal(c, False, 1)

            def low_part(c, H, k):
                dve.wait_ge(xhi_ready, 16 * c + 8 * H + k + 1)
                nc.vector.scalar_tensor_tensor(
                    out=xlo[:, k, HALF[H]], in0=x[:, k, HALF[H]], scalar=gains[:, pre_gain(c), k:k + 1],
                    in1=xhi[:, k, HALF[H]].bitcast(F32), op0=ALU.mult, op1=ALU.subtract).then_inc(xlo_ready, 1)

            def gate_part(e, f, H, ready, bank):
                dve.wait_ge(proj_ready, ready)
                if not isinstance(e, int) or e > 0:
                    dve.wait_ge(hlo_ready, e)
                nc.vector.tensor_tensor(scratch[:, 2 * H, :], psum[:, bank, 0:TH], rstd[:, HALF[H]],
                                        ALU.mult).then_inc(gate_scaled, 1)
                nc.vector.tensor_tensor(scratch[:, 2 * H + 1, :], psum[:, bank + 1, 0:TH], rstd[:, HALF[H]],
                                        ALU.mult).then_inc(proj_read, 1)
                dve.wait_ge(silu_done, e + 1)
                dve.wait_ge(proj_read, ready)
                nc.vector.tensor_tensor(scratch[:, 2 * H, :], scratch[:, 2 * H, :], scratch[:, 2 * H + 1, :],
                                        ALU.mult).then_inc(h_ready, 1)
                dve.wait_ge(hhi_ready, e + 1)
                nc.vector.tensor_tensor(h_lo[:, f, HALF[H]], scratch[:, 2 * H, :], h_hi[:, f, HALF[H]].bitcast(F32),
                                        ALU.subtract).then_inc(hlo_ready, 1)

            def rotate(job, rows, raw, raw_bank, table, dest, ready, done):
                a, b = scratch[rows, 2 * (job % 2), :], scratch[rows, 2 * (job % 2) + 1, :]
                dve.wait_ge(ready, job + 1)
                if job >= 2:
                    dve.wait_ge(done, job - 1)
                nc.vector.tensor_tensor(a, raw, table[0], ALU.mult)
                own_wait(own(nc.vector.tensor_tensor(b, psum[rows, raw_bank, 0:TH], table[1], ALU.mult)))
                nc.vector.tensor_tensor(dest, a, b, ALU.add).then_inc(done, 1)

            def attention_dve(name, between=None):
                items, done = ATT[name]
                base, obase = A0[name], O0[name]
                N = len(items)

                def maxima(n):
                    it, w, bank, part = items[n], items[n]["width"], n % 3, soft[:, n % 8, :]
                    dve.wait_ge(s_ready, base + n + 1)
                    heads = 2 if name == "swa" and it["kind"] == "prompt" else 1
                    scores = psum[:, bank, 0:heads * w].rearrange("p (d w) -> p d w", d=heads)
                    red = nc.vector.tensor_reduce(part[:, 0:heads], scores, AX_X, ALU.max, negate=True)
                    if name == "swa":
                        c = slice(it["h"], it["h"] + 3, 2) if it["kind"] == "prompt" else \
                            slice(CH + it["block"], CH + it["block"] + 1)
                        own_wait(own(red))
                        own_wait(own(nc.vector.tensor_tensor(part[:, 0:heads], part[:, 0:heads],
                                                             neg_sink[:, c], ALU.min)))
                        red = nc.vector.tensor_tensor(part[:, 4:4 + heads], part[:, 0:heads], sink[:, c],
                                                      ALU.add)
                    red.then_inc(max_ready, 1)

                def scale(n):
                    it, part = items[n], soft[:, n % 8, :]
                    heads = 2 if name == "swa" and it["kind"] == "prompt" else 1
                    slots = len(osb[name])
                    dve.wait_ge(pv_done, base + n + 1)
                    if it["to"][-1][0] >= slots:
                        dve.wait_ge(o_turned, obase + it["to"][-1][0] - slots + 1)
                    if name == "swa":
                        own_wait(own(nc.vector.tensor_tensor(part[:, 2:2 + heads], part[:, 2:2 + heads],
                                                             part[:, 4:4 + heads], ALU.add)))
                    own_wait(own(nc.vector.reciprocal(part[:, 2:2 + heads], part[:, 2:2 + heads])))
                    for k, e, d in it["to"]:
                        last = nc.vector.tensor_scalar(osb[name][k % slots][:, it["block"], HD * e:HD * (e + 1)],
                                                       psum[:, 5 + n % 2, HD * d:HD * (d + 1)],
                                                       part[:, 2 + d:3 + d], None, ALU.mult)
                    last.then_inc(o_scaled, 1)

                def head_outputs(k):
                    dve.wait_ge(o_hi, obase + k + 1)
                    for (hi, src), (lo, _) in zip(output_views(*done[k], xhi), output_views(*done[k], xlo)):
                        last = nc.vector.tensor_tensor(lo, src, hi.bitcast(F32), ALU.subtract)
                    last.then_inc(o_lo, 1)

                k = 0
                for n in range(N + 7):
                    if n < N:
                        maxima(n)
                    if between:
                        between(n)
                    if 5 <= n < N + 5:
                        scale(n - 5)
                    if k < len(done) and done[k][0] + 7 <= n:
                        head_outputs(k)
                        k += 1

            nc.vector.memset(eps[:], EPS).then_inc(gains_ready, 1)
            dve.wait_ge(gains_in, 16)
            for s, kind in enumerate(SUBS):
                factor = 0.5 if kind == "ffn" else 1.0
                nc.vector.tensor_scalar(post_gains[:, s, :], gains[:, pre_gain(s) + 1, :], factor, None,
                                        ALU.mult).then_inc(gains_ready, 1)
            dve.wait_ge(gains_ready, 7)
            for s, kind in enumerate(SUBS):
                g, n = G0[s], ffn_no(s)
                boundary(s)
                if kind == "ffn":
                    e0 = 2 * KF * n
                    split_group(dve, "dve", g + 2)
                    gate_part(e0, 0, 0, P0[s] + 1, 0)
                    gate_part(e0 + 1, 1, 0, P0[s] + 2, 4)
                    gate_part(e0 + 2, 0, 1, P0[s] + 3, 2)
                    gate_part(e0 + 3, 1, 1, P0[s] + 4, 6)
                    with dve.Fori(1, KF // 2 - 1) as i:
                        for e in range(2):
                            f = i * 2 + e
                            dve_split(dve, f + (g + 1), (g + e + 1) % 2, (KD, KD))
                            for H in range(2):
                                gate_part(f * 2 + (e0 + H), f, H, f * 2 + (P0[s] + H + 1), 4 * e + 2 * H)
                    for f in (KF - 2, KF - 1):
                        split_group(dve, "dve", g + f + 1)
                        for H in range(2):
                            gate_part(e0 + 2 * f + H, f, H, P0[s] + 2 * f + H + 1, 4 * (f % 2) + 2 * H)
                    split_group(dve, "dve", g + KF + 1)
                    split_group(dve, "dve", g + KF + 2)
                    with dve.Fori(1, KD // 2 - 1) as i:
                        for e in range(2):
                            dve_split(dve, i * 2 + (g + KF + 1 + e), (g + KF + 1 + e) % 2, (DU, DU))
                    split_group(dve, "dve", g + KF + KD - 1)
                    continue

                def project_out(event, f, H, bank, dests):
                    dve.wait_ge(proj_ready, P0[s] + event + 1)
                    for u in range(2):
                        if kind == "even" and f in (2, 3):
                            last = nc.vector.scalar_tensor_tensor(
                                out=dests[u][:, HALF[H]], in0=psum[:, bank + u, 0:TH], scalar=HEAD_SCALE,
                                in1=rstd[:, HALF[H]], op0=ALU.mult, op1=ALU.mult)
                        else:
                            last = nc.vector.tensor_tensor(dests[u][:, HALF[H]], psum[:, bank + u, 0:TH],
                                                           rstd[:, HALF[H]], ALU.mult)
                    last.then_inc(proj_read, 1)

                first = [(0, 0, 0, 0), (1, 1, 0, 4), (2, 0, 1, 2), (3, 1, 1, 6)]
                if kind == "even":
                    dests = [(cq[:, 0], cq[:, 1]), (ckv[:], kpe_raw[:])] + \
                        [(qkvb[:, 2 * j], qkvb[:, 2 * j + 1]) for j in range(6)]
                else:
                    dests = [(kC[:], vTC[:])] + [(qtC[:, 2 * j], qtC[:, 2 * j + 1]) for j in range(4)]
                split_group(dve, "dve", g + 2)
                for event, f, H, bank in first:
                    project_out(event, f, H, bank, dests[f])

                def later(f):
                    for H in range(2):
                        project_out(2 * f + H, f, H, 2 * H, dests[f])

                if kind == "even":
                    for f in (2, 3, 4):
                        split_group(dve, "dve", g + f + 1)
                        later(f)
                    for H in range(2):
                        dve.wait_ge(lat_std, H + 1)
                        own_wait(own(nc.vector.reciprocal(lat_rstd[:, :, HALF[H]], lat_rstd[:, :, HALF[H]])))
                        for t in range(3):
                            v = cq[:, t, HALF[H]] if t < 2 else ckv[:, HALF[H]]
                            nc.vector.scalar_tensor_tensor(
                                out=v, in0=v, scalar=lat_gains[:, t:t + 1], in1=lat_rstd[:, t // 2, HALF[H]],
                                op0=ALU.mult, op1=ALU.mult).then_inc(lat_norm, 1)
                    dve.wait_ge(lat_hi, 1)
                    nc.vector.tensor_tensor(ckv_lo[:, T:KEYS_A], ckv_cache[:], ckv_hi[:, T:KEYS_A].bitcast(F32),
                                            ALU.subtract).then_inc(lat_lo, 1)
                    for H in range(2):
                        dve.wait_ge(lat_norm, 3 * H + 3)
                        dve.wait_ge(lat_hi, 3 * H + 4)
                        for t in range(2):
                            nc.vector.tensor_tensor(cqn_lo[:, t, HALF[H]], cq[:, t, HALF[H]],
                                                    cqn_hi[:, t, HALF[H]].bitcast(F32), ALU.subtract).then_inc(lat_lo, 1)
                        nc.vector.tensor_tensor(ckv_lo[:, HALF[H]], ckv[:, HALF[H]], ckv_hi[:, HALF[H]].bitcast(F32),
                                                ALU.subtract).then_inc(lat_lo, 1)
                    for f in (5, 6, 7):
                        split_group(dve, "dve", g + f + 1)
                        later(f)
                    split_group(dve, "dve", g + 9)
                    dve.wait_ge(even_in, 16 * 5)
                    rows = slice(NOPE, QK)
                    for j in range(2 * NH + 2):
                        H = j % 2
                        raw = kpe_raw[rows, HALF[H]] if j < 2 else qtA[rows, j // 2 - 1, HALF[H]]
                        dest = kpe_all[rows, HALF[H]] if j < 2 else raw
                        rotate(j, rows, raw, 4 + j % 4, (ropeA[rows, 0, HALF[H]], ropeA[rows, 1, HALF[H]]), dest,
                               swapped, roped)
                    split_group(dve, "dve", g + 10)
                    for v in range(7):
                        dve.wait_ge(v_ready, v + 1)
                        if v == 0:
                            dve.wait_ge(roped, 2 * NH + 2)
                        nc.vector.tensor_copy(vA[:, v, :], psum[:, 4 + v % 4, :]).then_inc(v_copied, 1)
                    attention_dve("mla")
                    dve.wait_ge(rel_in, 16 * 11)
                    for h in range(NH):
                        nc.vector.tensor_scalar(hankel[:, h, :], hankel[:, h, :], rel_far[:, h:h + 1], None,
                                                ALU.subtract).then_inc(rel_shifted, 1)
                    for q in range(2):
                        nc.vector.tensor_scalar(hankelS[:, q, :], hankelS[:, q, :], far4[:, q:q + 1], None,
                                                ALU.subtract).then_inc(rel_shifted, 1)
                    for j in range(11):
                        if j % 2 == 0 and j < 5:
                            continue
                        hi, lo, src = band_result(j)
                        if lo is None:
                            dve.wait_ge(band_prep, j + 1)
                            nc.vector.tensor_copy(hi, src).then_inc(band_dve, 1)
                        else:
                            dve.wait_ge(band_act, j - 1)
                            nc.vector.tensor_tensor(lo, src, hi.bitcast(F32), ALU.subtract).then_inc(band_dve, 1)
                    attention_dve("band")
                else:
                    def rotate_c(j):
                        H = j % 2
                        raw = kC[:, HALF[H]] if j < 2 else qtC[:, j // 2 - 1, HALF[H]]
                        t = 2 if j < 2 else 0
                        rotate(j, slice(0, P), raw, 4 + j % 4 if j < 10 else 7, (ropeC[:, t, HALF[H]], ropeC[:, t + 1, HALF[H]]), raw,
                               c_swapped, c_roped)

                    dve.wait_ge(odd_in, 16 * 7)
                    nc.vector.tensor_scalar(neg_sink[:], sink[:], -1.0, None, ALU.mult).then_inc(sinks_ready, 1)
                    for f in (2, 3, 4):
                        split_group(dve, "dve", g + f + 1)
                        if f == 3:
                            for j in (0, 1):
                                rotate_c(j)
                            project_out(6, 3, 0, 0, dests[3])
                            for j in (2, 3):
                                rotate_c(j)
                            project_out(7, 3, 1, 2, dests[3])
                            for j in (4, 5):
                                rotate_c(j)
                        elif f == 4:
                            for H in range(2):
                                project_out(8 + H, 4, H, 2 * H, dests[4])
                                for j in (6 + 2 * H, 7 + 2 * H):
                                    rotate_c(j)
                        else:
                            later(f)
                    dve.wait_ge(sinks_ready, 1)
                    attention_dve("swa", lambda n: rotate_c(9 + n) if 1 <= n <= 8 else None)
                for j in range(1, 4):
                    split_group(dve, "dve", G0[s + 1] - 4 + j)
            boundary(len(SUBS))

        @block.gpsimd
        def _(pool):
            load = nc.gpsimd.dma_start
            s = 1
            pool.wait_ge(y_ready, 16 * s)
            rows = slice(NOPE, QK)
            load(ropeA[rows, :, :], ins["rope_mla"]).then_inc(even_in, 16)
            load(swapA[:], ins["swap_mla"]).then_inc(even_in, 16)
            load(rel_far[:], ins["rel_far"]).then_inc(even_in, 16)
            load(ckv_cache[:], ins["ckv_cache"]).then_inc(even_in, 16)
            load(kpe_all[rows, T:KEYS_A], ins["kpe_cache"]).then_inc(even_in, 16)
            nc.gpsimd.memset(ckv_hi[:, KEYS_A:KEYS_AP].bitcast(F32), 0.0).then_inc(pad_zero, 1)
            nc.gpsimd.memset(ckv_lo[:, KEYS_A:KEYS_AP].bitcast(F32), 0.0).then_inc(pad_zero, 1)
            pool.wait_ge(lat_norm, 6)
            pool.dma_start(outs["ckv"], ckv[:]).then_inc(latents_stored, 16)
            pool.wait_ge(proj_read, P0[s] + 16)
            pool.dma_start(outs["band_kv"], qkvb[:, 4:12, :]).then_inc(stored, 16)
            rel = ins["rel_rows"]
            load(hankel[:], bass.AP(rel.tensor, rel.offset + 32, [[1, P], [REL, NH], [1, 2 * P]])).then_inc(rel_in, 16)
            load(flips[:], ins["flips"]).then_inc(rel_in, 16)
            load(far4[:], ins["rel_far_sample"]).then_inc(rel_in, 16)
            load(mask_rawE[:], ins["mask"]).then_inc(mask_in, 16)
            pool.wait_ge(roped, 2)
            pool.dma_start(outs["kpe"], kpe_all[rows, 0:T]).then_inc(stored, 16)
            pool.wait_ge(lat_lo, 7)
            pool.wait_ge(latents_stored, 16)
            pool.wait_ge(even_in, 16 * 5)
            pool.wait_ge(pad_zero, 2)
            kpe = kpe_all[rows, :]
            load(ktA[rows, :, :], bass.AP(kpe.tensor, kpe.offset, [kpe.ap[0], [0, NH], kpe.ap[1]])).then_inc(kpe_spread, 16)
            for d in range(4):
                for cols, start in ((slice(0, DEC), 256), (slice(DEC, SK), 0)):
                    load(hankelS[32 * d:32 * d + 32, :, cols],
                         bass.AP(rel.tensor, rel.offset + d * REL + start,
                                 [[1, DEC], [4 * REL, 2], [1, cols.stop - cols.start]])).then_inc(rel_in, 16)
            pool.wait_ge(s_ready, A0["band"])
            load(vB_cache[:], ins["band_v_cache"]).then_inc(band_in, 16)
            load(kB_cache[:], ins["band_k_cache"]).then_inc(band_in, 16)
            s = 4
            pool.wait_ge(y_ready, 16 * s)
            load(ropeC[:], ins["rope_swa"]).then_inc(odd_in, 16)
            load(swapC[:], ins["swap_swa"]).then_inc(odd_in, 16)
            load(mask_rawC[:], ins["mask_swa"]).then_inc(odd_in, 16)
            load(vC_cache[:], ins["swa_v_cache"]).then_inc(odd_in, 16)
            load(kdup[:, :, T:KEYS_C], ins["swa_k_cache"]).then_inc(odd_in, 16)
            load(sink[:, 0:CH], ins["sinks"]).then_inc(odd_in, 16)
            load(sink[:, CH:CH + 4], ins["sinks_sample"]).then_inc(odd_in, 16)
            pool.wait_ge(proj_read, P0[s] + 4)
            pool.dma_start(outs["swa_v"], vTC[:]).then_inc(stored, 16)
            pool.wait_ge(c_roped, 2)
            for kv in range(CKV):
                for r in range(2):
                    pool.dma_start(kdup[64 * r:64 * r + 64, kv, 0:T], kC[64 * kv:64 * kv + 64, :]).then_inc(k_doubled, 16)
            pool.dma_start(outs["swa_k"], kC[:]).then_inc(stored, 16)
            pool.wait_ge(stored, 16 * 4)


def rotation(half, rows):
    inv = np.float32(500000.0) ** (-np.arange(half, dtype=np.float32) / np.float32(half))
    pos = np.concatenate([np.arange(SEQ), PAST + np.arange(DEC)]).astype(np.float32)
    ang = (pos[None, :] * inv.astype(np.float32)[:, None]).astype(np.float32)
    cos, sin = np.ones((rows, T), np.float32), np.zeros((rows, T), np.float32)
    cos[0:2 * half] = np.tile(np.cos(ang), (2, 1))
    sin[0:2 * half] = np.tile(np.sin(ang), (2, 1))
    return cos, sin


def partner(size, starts, half):
    m = np.zeros((size, size), np.float32)
    for a in starts:
        for i in range(half):
            m[a + half + i, a + i] = -1.0
            m[a + i, a + half + i] = 1.0
    return m


def tiled(w, columns):
    k = w.shape[0] // P
    return w[:, columns].reshape(k, P, -1, P).transpose(2, 1, 0, 3).reshape(-1, P, k * P)


def layouts(i):
    c = np.ascontiguousarray
    a = {}
    tok = np.concatenate([i["x_prompt"][0], i["x_sample"][0]], 0)
    a["x"] = c(tok.T.reshape(KD, P, T).transpose(1, 0, 2))
    a["gains"] = c(i["norm_g"].reshape(12, KD, P).transpose(2, 0, 1))
    a["lat_gains"] = c(np.concatenate([i["mla_q_norm"][0].reshape(2, P), i["mla_kv_norm"]], 0).T)
    a["ones"], a["ident"] = np.ones((P, P), np.float32), np.eye(P, dtype=np.float32)
    gu = [i[n].reshape(4, KD, P, KF, P).transpose(0, 3, 2, 1, 4).reshape(4, KF, P, D)
          for n in ("ffn_w_gate", "ffn_w_up")]
    a["w_gate_up"] = np.stack(gu, 2)
    a["w_down"] = c(i["ffn_w_down"].reshape(4, 2, DU, P, KD, P).transpose(0, 4, 1, 3, 2, 5)).reshape(4, KD, 2, P, UW)
    win = i["even_w_in"][0]
    pad = np.zeros((D, P), win.dtype)
    pad[:, NOPE:QK] = win[:, 384:416]
    wide = np.concatenate([win[:, 0:384], pad, win[:, 416:]], 1)
    a["even_in"] = c(tiled(wide, slice(None)).reshape(8, 2, P, D))
    uq = i["mla_w_uq"][0].reshape(2, P, 2, 4 * QK)
    a["mla_uq"] = c(uq.transpose(2, 1, 0, 3).reshape(2, P, 8 * QK))
    ukv = i["mla_w_ukv"][0]
    a["mla_ukv"] = c(np.concatenate([ukv, ukv.reshape(P, NH, P)[:, :, NOPE:].reshape(P, 512)], 1))
    a["even_out"] = c(tiled(i["even_w_out"][0], slice(None)).reshape(4, 2, P, D))
    wo = i["odd_w_in"][0]
    a["odd_in"] = c(tiled(np.concatenate([wo[:, D:], wo[:, 0:D]], 1), slice(None)).reshape(5, 2, P, D))
    a["odd_out"] = c(tiled(i["odd_w_out"][0], slice(None)).reshape(4, 2, P, D))
    a["ckv_cache"] = c(i["cache_mla_ckv"][0, 0].T)
    a["kpe_cache"] = c(i["cache_mla_kpe"][0, 0].T)
    a["band_k_cache"] = c(i["cache_band_k"][0, 0].reshape(PAST, 4, P).transpose(2, 1, 0))
    a["band_v_cache"] = c(i["cache_band_v"][0, 0].reshape(2, P, NH * HD).transpose(1, 0, 2))
    k = i["cache_swa_k"][0, 0].transpose(1, 2, 0)
    a["swa_k_cache"] = c(np.concatenate([k, k], 1).transpose(1, 0, 2))
    a["swa_v_cache"] = c(i["cache_swa_v"][0, 0].reshape(P, P))
    table = i["band_rel_bias"][0][:, ::-1]
    a["rel_rows"] = c(np.concatenate([np.repeat(table[:, 0:1], 159, 1), table[:, 0:256]], 1))
    a["rel_far"] = c(np.broadcast_to(table[:, 0][None, :], (P, NH)))
    a["rel_far_sample"] = c(np.repeat(table[:, 0].reshape(2, 4).T, 32, 0))
    mask = np.zeros((2, P, 2 * P), np.float32)
    mask[:, 0:64, 192:256] = NEG
    mask[1, 64:128, 0:64] = NEG
    a["mask"], a["mask_swa"] = mask[0], mask[1]
    sinks = i["swa_sinks"][0]
    a["sinks"] = c(np.broadcast_to(sinks[None, :], (P, CH)))
    a["sinks_sample"] = c(np.repeat(sinks.reshape(4, 4).T, 32, 0))
    flips = np.zeros((P, 2, P), np.float32)
    flips[:, 0] = np.eye(P)[::-1]
    for d in range(4):
        flips[32 * d:32 * d + 32, 1, 32 * d:32 * d + 32] = np.eye(32)[::-1]
    a["flips"] = flips
    cos, sin = rotation(ROPE // 2, ROPE)
    a["rope_mla"] = c(np.stack([cos, sin], 1))
    cos, sin = (np.tile(t, (2, 1)) for t in rotation(8, HD))
    a["rope_swa"] = c(np.stack([cos * np.float32(HEAD_SCALE), sin * np.float32(HEAD_SCALE), cos, sin], 1))
    a["swap_mla"] = partner(QK, [NOPE], ROPE // 2)
    a["swap_swa"] = partner(P, [0, HD], 8)
    return a


OUT_SHAPES = dict(y=(P, KD, T), ckv=(P, T), kpe=(ROPE, T), band_kv=(P, 8, T), swa_k=(P, T), swa_v=(P, T))


def kernel(**inputs):
    import concourse.bacc as bacc
    from concourse.bass_utils import run_bass_kernel_spmd

    arrays = layouts({k: np.asarray(v) for k, v in inputs.items()})
    nc = bacc.Bacc("TRN2", target_bir_lowering=False, num_devices=1)
    ins = {n: nc.dram_tensor("in_" + n, v.shape, F32, kind="ExternalInput").ap() for n, v in arrays.items()}
    outs = {n: nc.dram_tensor("out_" + n, s, F32, kind="ExternalOutput").ap() for n, s in OUT_SHAPES.items()}
    build(nc, ins, outs)
    r = run_bass_kernel_spmd(nc, [{"in_" + n: v for n, v in arrays.items()}], core_ids=[0]).results[0]
    y = r["out_y"].transpose(2, 1, 0).reshape(T, D)
    ckv, kpe = r["out_ckv"].T, r["out_kpe"].T
    kv = r["out_band_kv"].transpose(2, 1, 0).reshape(T, 2, NH, HD)
    ck, cv = r["out_swa_k"].T.reshape(T, CKV, HD), r["out_swa_v"].T.reshape(T, CKV, HD)
    c = np.ascontiguousarray
    prompt = (ckv[:SEQ], kpe[:SEQ], kv[:SEQ, 0], kv[:SEQ, 1], ck[SEQ - P:SEQ], cv[SEQ - P:SEQ])
    sample = (ckv[SEQ:], kpe[SEQ:], kv[SEQ:, 0], kv[SEQ:, 1], ck[SEQ:], cv[SEQ:])
    return (c(y[:SEQ])[None], c(y[SEQ:])[None], *(c(v)[None, None] for v in prompt + sample))
```
